# Optimizing a Trainium2 kernel written in Bass

```python
import jax, jax.numpy as jnp
from jax import lax
import numpy as np
import math

D_MODEL = 1024
BATCH = 1
SEQ = 256
DEPTH = 2

HEAD_DIM = 64
DIL_PATTERNS = ((128, 1), (512, 4), (2048, 16))
DIL_HEADS = 4
N_DIL_SUB = DIL_HEADS * len(DIL_PATTERNS)
DIL_QKV = N_DIL_SUB * HEAD_DIM
DIL_OUT = DIL_HEADS * HEAD_DIM
DIL_BLOCK = 64
WIN_HALF = 128
WIN_BLOCK = 128
WIN_Q = D_MODEL
WIN_Q_HEADS = WIN_Q // HEAD_DIM
WIN_KV_HEADS = 4
WIN_KV = WIN_KV_HEADS * HEAD_DIM
N_BRANCH = 2
SPLITS = (DIL_QKV, 2 * DIL_QKV, 3 * DIL_QKV,
          3 * DIL_QKV + WIN_Q, 3 * DIL_QKV + WIN_Q + WIN_KV, 3 * DIL_QKV + WIN_Q + 2 * WIN_KV)
IN_COLS = 3 * DIL_QKV + WIN_Q + 2 * WIN_KV + N_BRANCH * D_MODEL
N_EXPERTS = 16
CAPACITY_FACTOR = 2
D_EXPERT = 1024
RMS_EPS = 1e-6
NEG_INF = -1e30


def rmsnorm(x, g):
    xf = x.astype(jnp.float32)
    y = xf * lax.rsqrt(jnp.mean(xf * xf, axis=-1, keepdims=True) + RMS_EPS)
    return (y * g.astype(jnp.float32)).astype(x.dtype)

def alibi_slopes(n):
    return 2.0 ** (-8.0 * jnp.arange(1, n + 1, dtype=jnp.float32) / n)

def banded_attention(q, k, v, half, blk, slopes, pos_scale, sink=None):
    N, L, H, dh = q.shape
    Hk = k.shape[2]
    G = H // Hk
    nb = -(-L // blk)
    Lp = nb * blk
    pad = Lp - L
    qb = jnp.pad(q, ((0, 0), (0, pad), (0, 0), (0, 0))).reshape(N, nb, blk, Hk, G, dh)

    def key_blocks(t):
        tp = jnp.pad(t, ((0, 0), (blk, pad + blk), (0, 0), (0, 0)))
        return jnp.concatenate([
            tp[:, :Lp].reshape(N, nb, blk, Hk, dh),
            tp[:, blk:blk + Lp].reshape(N, nb, blk, Hk, dh),
            tp[:, 2 * blk:].reshape(N, nb, blk, Hk, dh)], axis=2)

    kb = key_blocks(k)
    vb = key_blocks(v)
    a = jnp.arange(blk)[:, None]
    b = jnp.arange(3 * blk)[None, :]
    rel = b - blk - a
    kpos = (jnp.arange(nb)[:, None, None] - 1) * blk + b[None]
    mask = (jnp.abs(rel) <= half)[None] & (kpos >= 0) & (kpos < L)
    bias = -slopes.astype(jnp.float32).reshape(Hk, G)[:, :, None, None] * \
        (pos_scale * jnp.abs(rel)).astype(jnp.float32)[None, None]
    s = jnp.einsum('nibkgd,nijkd->nikgbj', qb, kb).astype(jnp.float32) * (dh ** -0.5) + bias
    s = jnp.where(mask[None, :, None, None], s, NEG_INF)
    m = jnp.max(s, axis=-1)
    if sink is not None:
        sk = sink.astype(jnp.float32).reshape(Hk, G)[:, :, None]
        m = jnp.maximum(m, sk)
    p = jnp.exp(s - m[..., None])
    denom = jnp.sum(p, axis=-1)
    if sink is not None:
        denom = denom + jnp.exp(sk - m)
    p = p / denom[..., None]
    o = jnp.einsum('nikgbj,nijkd->nibkgd', p.astype(v.dtype), vb)
    o = o.reshape(N, Lp, H, dh)[:, :L]
    lse = jnp.moveaxis(m + jnp.log(denom), -1, 2).reshape(N, Lp, H)[:, :L]
    return o, lse

def dilated_mixture(q, k, v):
    B, S = q.shape[:2]
    slopes = alibi_slopes(N_DIL_SUB)
    outs, lses = [], []
    for g, (w, r) in enumerate(DIL_PATTERNS):
        sl = slice(g * DIL_HEADS, (g + 1) * DIL_HEADS)

        def strided(t):
            return t[:, :, sl].reshape(B, S // r, r, DIL_HEADS, HEAD_DIM).transpose(0, 2, 1, 3, 4) \
                .reshape(B * r, S // r, DIL_HEADS, HEAD_DIM)

        o, lse = banded_attention(strided(q), strided(k), strided(v), w // (2 * r), DIL_BLOCK,
                                  slopes[sl], r)
        outs.append(o.reshape(B, r, S // r, DIL_HEADS, HEAD_DIM).transpose(0, 2, 1, 3, 4)
                    .reshape(B, S, DIL_HEADS, HEAD_DIM))
        lses.append(lse.reshape(B, r, S // r, DIL_HEADS).transpose(0, 2, 1, 3).reshape(B, S, DIL_HEADS))
    wts = jax.nn.softmax(jnp.stack(lses, axis=0), axis=0)
    return jnp.sum(wts[..., None].astype(q.dtype) * jnp.stack(outs, axis=0), axis=0)

def hybrid_mixer(h, w_in, w_branch_a, w_branch_b, b_gate, sink_logit, w_out):
    B, S, D = h.shape
    proj = jnp.einsum('bsd,dc->bsc', h, w_in)
    qa, ka, va, qw, kw, vw, gates = jnp.split(proj, SPLITS, axis=-1)
    oa = dilated_mixture(qa.reshape(B, S, N_DIL_SUB, HEAD_DIM),
                         ka.reshape(B, S, N_DIL_SUB, HEAD_DIM),
                         va.reshape(B, S, N_DIL_SUB, HEAD_DIM))
    ya = jnp.einsum('bsc,cd->bsd', oa.reshape(B, S, DIL_OUT), w_branch_a)
    ob, _ = banded_attention(qw.reshape(B, S, WIN_Q_HEADS, HEAD_DIM),
                             kw.reshape(B, S, WIN_KV_HEADS, HEAD_DIM),
                             vw.reshape(B, S, WIN_KV_HEADS, HEAD_DIM),
                             WIN_HALF, WIN_BLOCK, alibi_slopes(WIN_Q_HEADS), 1, sink_logit)
    yb = jnp.einsum('bsc,cd->bsd', ob.reshape(B, S, WIN_Q), w_branch_b)
    g = jax.nn.sigmoid((gates + b_gate).astype(jnp.float32)).astype(h.dtype).reshape(B, S, N_BRANCH, D)
    merged = g[:, :, 0] * ya + g[:, :, 1] * yb
    return jnp.einsum('bsd,de->bse', merged, w_out)

def expert_choice_ffn(h, w_router, w_gate, w_up, w_down):
    B, S, D = h.shape
    cap = CAPACITY_FACTOR * S // N_EXPERTS
    aff = jax.nn.softmax(jnp.einsum('bsd,de->bse', h, w_router).astype(jnp.float32), axis=-1)
    gate, idx = lax.top_k(jnp.swapaxes(aff, 1, 2), cap)
    bidx = jnp.arange(B)[:, None, None]
    xe = h[bidx, idx]
    a = jnp.einsum('becd,edf->becf', xe, w_gate)
    u = jnp.einsum('becd,edf->becf', xe, w_up)
    ye = jnp.einsum('becf,efd->becd', jax.nn.silu(a) * u, w_down)
    return jnp.zeros_like(h).at[bidx, idx].add(gate[..., None].astype(h.dtype) * ye)

def first_inputs(seed: int = 0) -> dict:
    key = jax.random.key(seed)
    ks = jax.random.split(key, 14)
    f = jnp.float32
    return {
        "x": jax.random.normal(ks[0], (BATCH, SEQ, D_MODEL), f),
        "norm_mix": 1.0 + 0.02 * jax.random.normal(ks[1], (DEPTH, D_MODEL), f),
        "w_in": jax.random.normal(ks[2], (DEPTH, D_MODEL, IN_COLS), f) * D_MODEL ** -0.5,
        "w_branch_a": jax.random.normal(ks[3], (DEPTH, DIL_OUT, D_MODEL), f) * DIL_OUT ** -0.5,
        "w_branch_b": jax.random.normal(ks[4], (DEPTH, WIN_Q, D_MODEL), f) * WIN_Q ** -0.5,
        "b_gate": 0.1 * jax.random.normal(ks[5], (DEPTH, N_BRANCH * D_MODEL), f),
        "sink_logit": 0.5 * jax.random.normal(ks[6], (DEPTH, WIN_Q_HEADS), f),
        "w_out": jax.random.normal(ks[7], (DEPTH, D_MODEL, D_MODEL), f) * D_MODEL ** -0.5,
        "norm_ffn": 1.0 + 0.02 * jax.random.normal(ks[8], (DEPTH, D_MODEL), f),
        "w_router": jax.random.normal(ks[9], (DEPTH, D_MODEL, N_EXPERTS), f) * D_MODEL ** -0.5,
        "w_expert_gate": jax.random.normal(ks[10], (DEPTH, N_EXPERTS, D_MODEL, D_EXPERT), f) * D_MODEL ** -0.5,
        "w_expert_up": jax.random.normal(ks[11], (DEPTH, N_EXPERTS, D_MODEL, D_EXPERT), f) * D_MODEL ** -0.5,
        "w_expert_down": jax.random.normal(ks[12], (DEPTH, N_EXPERTS, D_EXPERT, D_MODEL), f) * D_EXPERT ** -0.5,
        "norm_final": 1.0 + 0.02 * jax.random.normal(ks[13], (D_MODEL,), f),
    }

def first_block(x, norm_mix, w_in, w_branch_a, w_branch_b, b_gate, sink_logit, w_out,
              norm_ffn, w_router, w_expert_gate, w_expert_up, w_expert_down, norm_final):
    h = x
    for l in range(DEPTH):
        h = h + hybrid_mixer(rmsnorm(h, norm_mix[l]), w_in[l], w_branch_a[l], w_branch_b[l],
                             b_gate[l], sink_logit[l], w_out[l])
        h = h + expert_choice_ffn(rmsnorm(h, norm_ffn[l]), w_router[l], w_expert_gate[l],
                                  w_expert_up[l], w_expert_down[l])
    return rmsnorm(h, norm_final)


N_MIXERS = 2
EPS = 1e-6
MEM_LEN = 256

MIX_WIDTH = D_MODEL
MEM_HEADS = 4
MEM_HEAD_DIM = 64
MEM_WIDTH = MEM_HEADS * MEM_HEAD_DIM
SEQ_WIDTH = MIX_WIDTH - MEM_WIDTH

A_HEAD_DIM = 64
A_HEADS = SEQ_WIDTH // A_HEAD_DIM
A_KV_RANK = 256
IDX_HEADS = 8
IDX_DIM = 64
IDX_TOPK_MAX = 256
Q_BLOCK = 128

REL_BUCKETS = 32
REL_MAX_DIST = 128

SSM_HEAD_DIM = 64
SSM_HEADS = SEQ_WIDTH // SSM_HEAD_DIM
SSM_GROUPS = 2
HEADS_PER_GROUP = SSM_HEADS // SSM_GROUPS
SSM_STATE = 128
CONV_WIDTH = 4
SSD_CHUNK = 128
CONV_DIM = SEQ_WIDTH + 2 * SSM_GROUPS * SSM_STATE

PEER_HEADS = 8
PEER_KEYS = 128
PEER_EXPERTS = PEER_KEYS * PEER_KEYS
PEER_QDIM = 256
PEER_TOPK = 16
TOKEN_BLOCK = 128

N_A_LAYERS = (DEPTH + 1) // 2
N_B_LAYERS = DEPTH // 2

def _split_points(widths):
    pts, acc = [], 0
    for w in widths[:-1]:
        acc += w
        pts.append(acc)
    return pts

A_WIDTHS = [SEQ_WIDTH, A_KV_RANK, IDX_HEADS * IDX_DIM, IDX_DIM, IDX_HEADS, MEM_WIDTH]
B_WIDTHS = [SEQ_WIDTH, CONV_DIM, SSM_HEADS, MEM_WIDTH]
A_IN = sum(A_WIDTHS)
B_IN = sum(B_WIDTHS)
A_SPLITS = _split_points(A_WIDTHS)
B_SPLITS = _split_points(B_WIDTHS)


def rms_norm(x, g):
    xf = x.astype(jnp.float32)
    y = xf * lax.rsqrt(jnp.mean(xf * xf, axis=-1, keepdims=True) + EPS)
    return (y * g.astype(jnp.float32)).astype(x.dtype)

def t5_causal_bucket(dist):
    n = jnp.maximum(dist, 0)
    max_exact = REL_BUCKETS // 2
    nf = jnp.maximum(n, max_exact).astype(jnp.float32)
    large = max_exact + (jnp.log(nf / max_exact) / math.log(REL_MAX_DIST / max_exact)
                         * (REL_BUCKETS - max_exact)).astype(jnp.int32)
    large = jnp.minimum(large, REL_BUCKETS - 1)
    return jnp.where(n < max_exact, n, large)

def memory_attention(q, mem_n, w_kv):
    b, s, _ = q.shape
    k, v = jnp.split(mem_n @ w_kv, 2, axis=-1)
    q = q.reshape(b, s, MEM_HEADS, MEM_HEAD_DIM)
    k = k.reshape(b, -1, MEM_HEADS, MEM_HEAD_DIM)
    v = v.reshape(b, -1, MEM_HEADS, MEM_HEAD_DIM)
    logits = jnp.einsum('bqhd,bmhd->bhqm', q, k).astype(jnp.float32) * (MEM_HEAD_DIM ** -0.5)
    p = jax.nn.softmax(logits, axis=-1).astype(v.dtype)
    o = jnp.einsum('bhqm,bmhd->bqhd', p, v)
    return o.reshape(b, s, MEM_WIDTH)

def dsa_attention(q, c_kv, iq, ik, iw, w_uk, w_uv, rel_bias):
    b, s = c_kv.shape[:2]
    topk = min(IDX_TOPK_MAX, s // 4)
    n_blk = s // Q_BLOCK
    key_pos = jnp.arange(s, dtype=jnp.int32)

    def block(i):
        t0 = i * Q_BLOCK
        qb = lax.dynamic_slice_in_dim(q, t0, Q_BLOCK, axis=1)
        iqb = lax.dynamic_slice_in_dim(iq, t0, Q_BLOCK, axis=1)
        iwb = lax.dynamic_slice_in_dim(iw, t0, Q_BLOCK, axis=1)
        q_pos = t0 + jnp.arange(Q_BLOCK, dtype=jnp.int32)
        rel = jax.nn.relu(jnp.einsum('bqhd,bsd->bqhs', iqb, ik).astype(jnp.float32) * (IDX_DIM ** -0.5))
        score = jnp.einsum('bqhs,bqh->bqs', rel, iwb.astype(jnp.float32) * (IDX_HEADS ** -0.5))
        causal = key_pos[None, :] <= q_pos[:, None]
        score = jnp.where(causal[None], score, -jnp.inf)
        _, sel = lax.top_k(score, topk)
        c_sel = jax.vmap(lambda c, idx: c[idx])(c_kv, sel)
        q_lat = jnp.einsum('bqhd,hcd->bqhc', qb, w_uk)
        logits = jnp.einsum('bqhc,bqkc->bhqk', q_lat, c_sel).astype(jnp.float32) * (A_HEAD_DIM ** -0.5)
        dist = q_pos[None, :, None] - sel
        bias = rel_bias[t5_causal_bucket(dist)]
        logits = logits + jnp.moveaxis(bias, -1, 1).astype(jnp.float32)
        logits = jnp.where((dist >= 0)[:, None], logits, -jnp.inf)
        p = jax.nn.softmax(logits, axis=-1).astype(c_sel.dtype)
        o_lat = jnp.einsum('bhqk,bqkc->bqhc', p, c_sel)
        o = jnp.einsum('bqhc,hcd->bqhd', o_lat, w_uv)
        return o.reshape(b, Q_BLOCK, SEQ_WIDTH)

    out = lax.map(block, jnp.arange(n_blk))
    return jnp.moveaxis(out, 0, 1).reshape(b, s, SEQ_WIDTH)

def causal_depthwise_conv(x, w, bias):
    c = x.shape[-1]
    y = lax.conv_general_dilated(x, w[:, None, :].astype(x.dtype), window_strides=(1,),
                                 padding=[(CONV_WIDTH - 1, 0)],
                                 dimension_numbers=('NWC', 'WIO', 'NWC'),
                                 feature_group_count=c)
    return y + bias.astype(x.dtype)

def ssd_scan(xh, dt, a, bm, cm):
    b, s, g, r, p = xh.shape
    n = bm.shape[-1]
    l = SSD_CHUNK
    c = s // l
    f32 = jnp.float32
    x = (xh.astype(f32) * dt[..., None]).reshape(b, c, l, g, r, p)
    da = (dt * a).reshape(b, c, l, g, r)
    bc = bm.astype(f32).reshape(b, c, l, g, n)
    cc = cm.astype(f32).reshape(b, c, l, g, n)
    a_cs = jnp.cumsum(da, axis=2)
    seg = a_cs[:, :, :, None] - a_cs[:, :, None, :]
    tri = jnp.tril(jnp.ones((l, l), dtype=bool))[None, None, :, :, None, None]
    decay = jnp.exp(jnp.where(tri, seg, -jnp.inf))
    cb = jnp.einsum('bclgn,bcsgn->bclsg', cc, bc)
    y_diag = jnp.einsum('bclsg,bclsgr,bcsgrp->bclgrp', cb, decay, x)
    decay_to_end = jnp.exp(a_cs[:, :, -1:] - a_cs)
    states = jnp.einsum('bclgn,bclgr,bclgrp->bcgrpn', bc, decay_to_end, x)
    chunk_decay = jnp.exp(a_cs[:, :, -1])

    def step(h, inp):
        st, dec = inp
        return h * dec[..., None, None] + st, h

    h0 = jnp.zeros((b, g, r, p, n), f32)
    _, h_prev = lax.scan(step, h0, (jnp.moveaxis(states, 1, 0), jnp.moveaxis(chunk_decay, 1, 0)))
    h_prev = jnp.moveaxis(h_prev, 0, 1)
    y_off = jnp.einsum('bclgn,bcgrpn,bclgr->bclgrp', cc, h_prev, jnp.exp(a_cs))
    return (y_diag + y_off).reshape(b, s, g, r, p)

def mamba2_mixer(z, xbc, dt_raw, conv_w, conv_b, dt_bias, a_log, d_skip, out_norm):
    b, s, _ = z.shape
    xbc = jax.nn.silu(causal_depthwise_conv(xbc, conv_w, conv_b))
    xs, bm, cm = jnp.split(xbc, [SEQ_WIDTH, SEQ_WIDTH + SSM_GROUPS * SSM_STATE], axis=-1)
    xh = xs.reshape(b, s, SSM_GROUPS, HEADS_PER_GROUP, SSM_HEAD_DIM)
    bm = bm.reshape(b, s, SSM_GROUPS, SSM_STATE)
    cm = cm.reshape(b, s, SSM_GROUPS, SSM_STATE)
    dt = jax.nn.softplus(dt_raw.astype(jnp.float32) + dt_bias.astype(jnp.float32))
    dt = dt.reshape(b, s, SSM_GROUPS, HEADS_PER_GROUP)
    a = -jnp.exp(a_log.astype(jnp.float32)).reshape(SSM_GROUPS, HEADS_PER_GROUP)
    d = d_skip.astype(jnp.float32).reshape(SSM_GROUPS, HEADS_PER_GROUP)
    y = ssd_scan(xh, dt, a, bm, cm) + xh.astype(jnp.float32) * d[..., None]
    y = y.reshape(b, s, SEQ_WIDTH) * jax.nn.silu(z.astype(jnp.float32))
    return rms_norm(y, out_norm).astype(z.dtype)

def peer_ffn(h, w_q, sub_keys, u, v):
    b, s, d = h.shape
    q = (h @ w_q).reshape(b, s, PEER_HEADS, 2, PEER_QDIM // 2)
    scores = jnp.einsum('bshic,ikc->bshik', q, sub_keys).astype(jnp.float32)
    top_s, top_i = lax.top_k(scores, PEER_TOPK)
    cand_s = top_s[..., 0, :, None] + top_s[..., 1, None, :]
    cand_i = top_i[..., 0, :, None] * PEER_KEYS + top_i[..., 1, None, :]
    cand_s = cand_s.reshape(b, s, PEER_HEADS, PEER_TOPK * PEER_TOPK)
    cand_i = cand_i.reshape(b, s, PEER_HEADS, PEER_TOPK * PEER_TOPK)
    best_s, pos = lax.top_k(cand_s, PEER_TOPK)
    expert = jnp.take_along_axis(cand_i, pos, axis=-1)
    gate = jax.nn.softmax(best_s, axis=-1).astype(h.dtype)
    nb = (b * s) // TOKEN_BLOCK
    hb = h.reshape(nb, TOKEN_BLOCK, d)
    eb = expert.reshape(nb, TOKEN_BLOCK, PEER_HEADS, PEER_TOPK)
    gb = gate.reshape(nb, TOKEN_BLOCK, PEER_HEADS, PEER_TOPK)

    def block(args):
        xt, et, gt = args
        act = jax.nn.gelu(jnp.einsum('td,thkd->thk', xt, u[et]), approximate=False)
        return jnp.einsum('thk,thkd->td', act * gt, v[et])

    out = lax.map(block, (hb, eb, gb))
    return out.reshape(b, s, d)

def second_inputs(seed: int = 0) -> dict:
    key = jax.random.key(seed)
    ks = jax.random.split(key, 26)
    f32 = jnp.float32
    nA, nB = N_A_LAYERS, N_B_LAYERS

    def nrm(k, shape, scale):
        return jax.random.normal(k, shape, f32) * scale

    def gain(k, shape):
        return 1.0 + 0.05 * jax.random.normal(k, shape, f32)

    dt0 = jnp.exp(jax.random.uniform(ks[14], (nB, SSM_HEADS), f32, math.log(1e-3), math.log(1e-1)))
    return {
        "x": jax.random.normal(ks[0], (BATCH, SEQ, D_MODEL), f32),
        "mem": jax.random.normal(ks[1], (BATCH, MEM_LEN, D_MODEL), f32),
        "mem_norm": gain(ks[2], (D_MODEL,)),
        "rel_bias": nrm(ks[3], (REL_BUCKETS, A_HEADS), 0.5),
        "mix_norm": gain(ks[4], (DEPTH, D_MODEL)),
        "ffn_norm": gain(ks[5], (DEPTH, D_MODEL)),
        "final_norm": gain(ks[6], (D_MODEL,)),
        "w_o": nrm(ks[7], (DEPTH, MIX_WIDTH, D_MODEL), MIX_WIDTH ** -0.5),
        "w_mem_kv": nrm(ks[8], (DEPTH, D_MODEL, 2 * MEM_WIDTH), D_MODEL ** -0.5),
        "a_w_in": nrm(ks[9], (nA, D_MODEL, A_IN), D_MODEL ** -0.5),
        "a_kv_norm": gain(ks[10], (nA, A_KV_RANK)),
        "a_w_uk": nrm(ks[11], (nA, A_HEADS, A_KV_RANK, A_HEAD_DIM), A_KV_RANK ** -0.5),
        "a_w_uv": nrm(ks[12], (nA, A_HEADS, A_KV_RANK, A_HEAD_DIM), A_KV_RANK ** -0.5),
        "b_w_in": nrm(ks[13], (nB, D_MODEL, B_IN), D_MODEL ** -0.5),
        "b_conv_w": nrm(ks[15], (nB, CONV_WIDTH, CONV_DIM), CONV_WIDTH ** -0.5),
        "b_conv_b": nrm(ks[16], (nB, CONV_DIM), 0.02),
        "b_dt_bias": dt0 + jnp.log(-jnp.expm1(-dt0)),
        "b_a_log": jnp.log(jax.random.uniform(ks[17], (nB, SSM_HEADS), f32, 1.0, 16.0)),
        "b_d_skip": 1.0 + 0.1 * jax.random.normal(ks[18], (nB, SSM_HEADS), f32),
        "b_out_norm": gain(ks[19], (nB, SEQ_WIDTH)),
        "peer_w_q": nrm(ks[20], (DEPTH, D_MODEL, PEER_HEADS * PEER_QDIM), D_MODEL ** -0.5),
        "peer_sub_keys": nrm(ks[21], (DEPTH, 2, PEER_KEYS, PEER_QDIM // 2), (PEER_QDIM // 2) ** -0.5),
        "peer_u": nrm(ks[22], (DEPTH, PEER_EXPERTS, D_MODEL), D_MODEL ** -0.5),
        "peer_v": nrm(ks[23], (DEPTH, PEER_EXPERTS, D_MODEL), D_MODEL ** -0.5),
    }

def second_block(x, mem, mem_norm, rel_bias, mix_norm, ffn_norm, final_norm, w_o, w_mem_kv,
              a_w_in, a_kv_norm, a_w_uk, a_w_uv,
              b_w_in, b_conv_w, b_conv_b, b_dt_bias, b_a_log, b_d_skip, b_out_norm,
              peer_w_q, peer_sub_keys, peer_u, peer_v):
    b, s, _ = x.shape
    mem_n = rms_norm(mem, mem_norm)
    for i in range(DEPTH):
        h = rms_norm(x, mix_norm[i])
        j = i // N_MIXERS
        if i % N_MIXERS == 0:
            q, c_kv, iq, ik, iw, q_mem = jnp.split(h @ a_w_in[j], A_SPLITS, axis=-1)
            c_kv = rms_norm(c_kv, a_kv_norm[j])
            seq_out = dsa_attention(q.reshape(b, s, A_HEADS, A_HEAD_DIM), c_kv,
                                    iq.reshape(b, s, IDX_HEADS, IDX_DIM), ik, iw,
                                    a_w_uk[j], a_w_uv[j], rel_bias)
        else:
            z, xbc, dt_raw, q_mem = jnp.split(h @ b_w_in[j], B_SPLITS, axis=-1)
            seq_out = mamba2_mixer(z, xbc, dt_raw, b_conv_w[j], b_conv_b[j], b_dt_bias[j],
                                   b_a_log[j], b_d_skip[j], b_out_norm[j])
        mem_out = memory_attention(q_mem, mem_n, w_mem_kv[i])
        x = x + jnp.concatenate([seq_out, mem_out], axis=-1) @ w_o[i]
        x = x + peer_ffn(rms_norm(x, ffn_norm[i]), peer_w_q[i], peer_sub_keys[i], peer_u[i], peer_v[i])
    return rms_norm(x, final_norm)


def setup_inputs(seed=0):
    out = dict(first_inputs(seed))
    for name, value in second_inputs(seed + 1).items():
        if name != "x":
            out[name + "_2"] = value
    return out


def reference(
    x, norm_mix, w_in, w_branch_a, w_branch_b, b_gate, sink_logit, w_out, norm_ffn, w_router,
    w_expert_gate, w_expert_up, w_expert_down, norm_final, mem_2, mem_norm_2, rel_bias_2,
    mix_norm_2, ffn_norm_2, final_norm_2, w_o_2, w_mem_kv_2, a_w_in_2, a_kv_norm_2, a_w_uk_2,
    a_w_uv_2, b_w_in_2, b_conv_w_2, b_conv_b_2, b_dt_bias_2, b_a_log_2, b_d_skip_2,
    b_out_norm_2, peer_w_q_2, peer_sub_keys_2, peer_u_2, peer_v_2,
):
    x = first_block(
        x, norm_mix, w_in, w_branch_a, w_branch_b, b_gate, sink_logit, w_out, norm_ffn,
        w_router, w_expert_gate, w_expert_up, w_expert_down, norm_final,
    )
    return second_block(
        x, mem_2, mem_norm_2, rel_bias_2, mix_norm_2, ffn_norm_2, final_norm_2, w_o_2,
        w_mem_kv_2, a_w_in_2, a_kv_norm_2, a_w_uk_2, a_w_uv_2, b_w_in_2, b_conv_w_2, b_conv_b_2,
        b_dt_bias_2, b_a_log_2, b_d_skip_2, b_out_norm_2, peer_w_q_2, peer_sub_keys_2, peer_u_2,
        peer_v_2,
    )


_drawn_inputs = setup_inputs


def setup_inputs(seed=0):
    import zlib

    import numpy as np

    out = dict(_drawn_inputs(seed))
    spreads = {}
    factors = {'mem_norm_2': 8.0,
     'ffn_norm_2': 8.0,
     'a_kv_norm_2': 2.77,
     'b_conv_b_2': 9.134,
     'peer_u_2': 2.906,
     'b_d_skip_2': 3.565,
     'b_out_norm_2': 4.943}
    for name, (base, spread) in spreads.items():
        noise = np.random.default_rng([zlib.crc32(name.encode()), seed]).standard_normal(out[name].shape)
        drawn = base * np.exp(spread * noise) if base else spread * noise
        out[name] = __import__('jax').numpy.asarray(drawn.astype(out[name].dtype))
    for name, factor in factors.items():
        out[name] = (out[name] * factor).astype(out[name].dtype)
    return out
```

```python
from contextlib import ExitStack

import concourse.bass as bass
from concourse import mybir

F32 = mybir.dt.float32
U32 = mybir.dt.uint32
ALU = mybir.AluOpType
ACT = mybir.ActivationFunctionType
AX_X = mybir.AxisListType.X
P = 128
NEG = -1.0e30
LOW = -3.0e38

PF = {}
PR = {}
CO = {}


def _layout():
    at = 0
    for name, n in (("norm_mix0", 8), ("norm_mix1", 8), ("norm_ffn0", 8), ("norm_ffn1", 8),
                    ("mix20", 8), ("mix21", 8), ("ffn20", 8), ("ffn21", 8), ("mem", 8),
                    ("bgate0", 16), ("bgate1", 16), ("conv", 40), ("convb", 10), ("kvn", 2), ("outn", 6)):
        PF[name] = (at, at + n)
        at += n
    PF["all"] = (0, at)
    at = 0
    for name, n in (("final", 1024), ("final2", 1024), ("ffn20", 1024), ("ffn21", 1024), ("kvn", 256),
                    ("sink0", 16), ("sink1", 16), ("dtb", 12), ("alog", 12), ("dskip", 12)):
        PR[name] = (at, at + n)
        at += n
    PR["all"] = (0, at)
    at = 0
    for name, n in (("ident", 128), ("uinc", 128), ("ustr", 128), ("ones", 128), ("causal", 512), ("mt", 128),
                    ("iota", 32), ("nhalf", 2)):
        CO[name] = (at, at + n)
        at += n
    CO["all"] = (0, at)


_layout()


class Queue:

    def __init__(self, sem):
        self.sem, self.n, self.items, self.seen = sem, 0, [], {}

    def wait(self, *toks):
        for t in toks:
            if t is None:
                continue
            if not (len(t) == 2 and isinstance(t[1], int)):
                self.wait(*t)
                continue
            sem, v = t
            if v > self.seen.get(id(sem), 0):
                self.seen[id(sem)] = v
                self.items.append(lambda e, sem=sem, v=v: e.wait_ge(sem, v))

    def last(self):
        return (self.sem, self.n) if self.n else None

    def op(self, fn, *toks):
        self.wait(*toks)
        self.n += 1
        self.items.append(lambda e, sem=self.sem: fn(e).then_inc(sem, 1))
        return (self.sem, self.n)

    def play(self, e):
        for it in self.items:
            it(e)


class Serial(Queue):

    def op(self, fn, *toks):
        return Queue.op(self, fn, self.last(), *toks)


class Slot:

    def __init__(self, buf, sem, gsem=None):
        self.buf, self.sem, self.cnt, self.free = buf, sem, 0, []
        self.gsem, self.gcnt = gsem, 0

    def load(self, q, pairs, *toks):
        q.wait(self.free, *toks)
        for dst, src in pairs:
            q.items.append(lambda e, dst=dst, src=src: e.dma_start(dst, src).then_inc(self.sem, 16))
        self.cnt += 16 * len(pairs)
        self.free = []
        return (self.sem, self.cnt)


class Late:
    def __init__(self, f):
        self.f, self.v = f, None

    def get(self):
        if self.v is None:
            self.v = self.f()
        return self.v

    def __iter__(self):
        return iter(self.get())

    def __getitem__(self, k):
        return self.get()[k]


class Ring:
    def __init__(self, slots):
        self.slots, self.n = slots, 0

    def get(self):
        self.n += 1
        s = self.slots[(self.n - 1) % len(self.slots)]
        assert s.cnt + s.gcnt == 0 or s.free
        return s


class Banks:
    def __init__(self, bufs):
        self.idle = [Bank(b) for b in bufs]

    def get(self):
        return self.idle.pop(0)

    def put(self, b, *toks):
        b.free = list(toks)
        self.idle.append(b)


class Bank:
    def __init__(self, buf):
        self.buf, self.free = buf, []

    def __getitem__(self, k):
        return self.buf[k]


def program(nc, I, out):
    ctx = ExitStack()
    with ctx:
        def sb(name, shape, dt=F32):
            return ctx.enter_context(nc.sbuf_tensor(name, shape, dt))

        def sem(name):
            return ctx.enter_context(nc.semaphore(name))

        co = sb("co", [P, CO["all"][1]])
        pf = sb("pf", [P, PF["all"][1]])
        X = sb("X", [P, 2, 1024])
        Y = sb("Y", [P, 2, 1024])
        HT = sb("HT", [P, 8, 256])
        sm = sb("sm", [P, 512])
        wbuf = sb("wbuf", [P, 6, 4096])
        cbuf = sb("cbuf", [P, 2, 1536])
        ar = sb("ar", [P, 16384])
        bc = sb("bc", [P, 324])
        arU = ar[:, :].bitcast(U32)
        PS = Banks([ctx.enter_context(nc.psum_tensor(f"ps{i}", [P, 512], F32)) for i in range(8)])
        zd = nc.dram_tensor("zd", (12, 128, 512), F32, kind="Internal").ap()

        V, A, G, T = Serial(sem("sV")), Serial(sem("sA")), Serial(sem("sG")), Queue(sem("sT"))
        S = Queue(sem("sS"))
        WR = Ring([Slot(wbuf[:, k, :], sem(f"w{k}"), sem(f"g{k}")) for k in range(6)])
        CR = Ring([Slot(cbuf[:, k, :], sem(f"c{k}")) for k in range(2)])
        one = [Slot(None, sem(f"m{k}")) for k in range(12)]
        s_out = sem("s_out")

        def C(name):
            return co[:, CO[name][0]:CO[name][1]]

        ident = C("ident")

        def gain(name, c):
            return pf[:, PF[name][0] + c:PF[name][0] + c + 1]

        def cp(E, o, i, *w):
            if E is A:
                return E.op(lambda e: e.copy(o, i), *w)
            return E.op(lambda e: e.tensor_copy(o, i), *w)

        def tt(E, o, a, b, op, *w):
            return E.op(lambda e: e.tensor_tensor(o, a, b, op), *w)

        def ts(o, i, s1, s2, op0, op1, *w):
            if op1 is None:
                return V.op(lambda e: e.tensor_scalar(o, i, s1, None, op0), *w)
            return V.op(lambda e: e.tensor_scalar(o, i, s1, s2, op0, op1), *w)

        def stt(o, i, s, i1, op0, op1, *w):
            return V.op(lambda e: e.scalar_tensor_tensor(out=o, in0=i, scalar=s, in1=i1, op0=op0, op1=op1), *w)

        def ttr(o, a, b, op0, op1, init, acc, *w):
            return V.op(lambda e: e.tensor_tensor_reduce(o, a, b, 1.0, init, op0, op1, acc), *w)

        def act(o, i, f, *w, bias=None, scale=None, acc=None):
            kw = {}
            if bias is not None:
                kw["bias"] = bias
            if scale is not None:
                kw["scale"] = scale
            if acc is not None:
                kw["accum_out"] = acc
            return A.op(lambda e: e.activation(o, i, f, **kw), *w)

        def red(o, i, op, *w):
            return V.op(lambda e: e.tensor_reduce(o, i, AX_X, op), *w)

        def recip(o, i, *w):
            return V.op(lambda e: e.reciprocal(o, i), *w)

        def mm(groups, *w):
            def f(e):
                for o, pairs in groups:
                    for n, (l, r) in enumerate(pairs):
                        m = e.matmul(o, l, r, start=(n == 0), stop=(n == len(pairs) - 1))
                return m
            return T.op(f, *w)

        def tr(jobs, *w):
            def f(e):
                for o, i in jobs:
                    m = e.transpose(o, i, ident[0:i.shape[0], 0:i.shape[0]])
                return m
            return T.op(f, *w)

        def small(a, n):
            return sm[:, a:a + n]

        t_co = one[0].load(S, [(co[:, :], I["co"]), (pf[:, :], I["pf"]),
                               (bc[:, :], I["pr"][0:1, PR["kvn"][0]:PR["all"][1]].to_broadcast([P, 324]))])
        for i in range(2):
            t_x = one[1].load(S, [(X[:, i, :], I["x"][0, 128 * i:128 * i + 128, :])])
        for E in (V, A, G, T):
            E.wait(t_co)
        V.wait(t_x)
        A.wait(t_x)

        def B(name):
            a, b = PR[name]
            o = PR["kvn"][0]
            return bc[:, a - o:b - o]

        def rstd(src, n, cols, junk, *w):
            ss = small(0, len(src))
            for i, s_ in enumerate(src):
                t = act(junk[i], s_, ACT.Square, w, acc=ss[:, i:i + 1])
            t = ts(cols, ss, 1.0 / n, 1e-6, ALU.mult, ALU.add, t)
            nh = C("nhalf")[:, 0:len(src)]
            return G.op(lambda e: e.tensor_tensor(cols, cols, nh, ALU.pow), t)

        def to_T(dst, src, nch, gname, *w):
            toks = []
            for c in range(0, nch, 2):
                b = PS.get()
                t = tr([(b[:, (2 * k + i) * 128:(2 * k + i) * 128 + 128],
                         src[:, i, (c + k) * 128:(c + k) * 128 + 128]) for k in range(2) for i in range(2)],
                       w, b.free)
                if gname is None:
                    E = V if c % 4 else A
                    u = [cp(E, dst[:, c:c + 2, :], b[:, :].rearrange("p (k t) -> p k t", k=2), t)]
                else:
                    u = []
                    for k in range(2):
                        o, g_ = dst[:, c + k, :], gain(gname, c + k)
                        if c % 4:
                            u.append(ts(o, b[:, 256 * k:256 * k + 256], g_, None, ALU.mult, None, t))
                        else:
                            u.append(act(o, b[:, 256 * k:256 * k + 256], ACT.Copy, t, scale=g_))
                PS.put(b, *u)
                toks += u
            return toks

        def norm(gname, src=X, *w):
            w = [w, T.last(), V.last(), A.last()]
            r = small(8, 2)
            t = rstd([src[:, 0, :], src[:, 1, :]], 1024, r, [Y[:, 0, :], Y[:, 1, :]], w)
            a = ts(Y[:, 0, :], src[:, 0, :], r[:, 0:1], None, ALU.mult, None, t)
            b = act(Y[:, 1, :], src[:, 1, :], ACT.Copy, t, scale=r[:, 1:2])
            return to_T(HT, Y, 8, gname, a, b)

        def wload(src, nk, n, *w):
            sl = WR.get()
            v = sl.buf[:, 0:nk * n].rearrange("p (k n) -> p k n", k=nk)
            t = sl.load(S, [(v, src.rearrange("(k p) n -> p k n", p=P))], *w)
            return sl, v, t

        def evac_any(o, i, n, scale, *w):
            if n % 2:
                return ts(o, i, scale, None, ALU.mult, None, *w) if scale != 1.0 else cp(V, o, i, *w)
            return act(o, i, ACT.Copy, *w, scale=scale) if scale != 1.0 else cp(A, o, i, *w)

        cnt = [0]

        def proj_T(sl_v_t, lhs_of, nchunk, K, rhsT, dsts, w, fin=None):
            sl, v, tw = sl_v_t
            out_ = []
            for j in range(0, nchunk, 2):
                b = PS.get()
                m = min(2, nchunk - j)
                t = mm([(b[:, 256 * k:256 * k + 256], [(lhs_of(v, c, j + k), rhsT[:, c, :]) for c in range(K)])
                        for k in range(m)], tw, w, b.free)
                cnt[0] += 1
                o, sc = dsts(j, m)
                if fin is not None:
                    u = fin(j, m, b, t)
                else:
                    u = evac_any(o, b[:, 0:256 * m].rearrange("p (k t) -> p k t", k=m), cnt[0], sc, t)
                PS.put(b, u)
                out_.append(u)
            return t, out_

        def proj_N(sl_v_t, c0, n, K, lT, dst, w):
            sl, v, tw = sl_v_t
            out_ = []
            for i in range(2):
                b = PS.get()
                t = mm([(b[:, 0:n], [(lT[:, c, 128 * i:128 * i + 128], v[:, c, c0:c0 + n]) for c in range(K)])],
                       tw, w, b.free)
                cnt[0] += 1
                u = evac_any(dst(i), b[:, 0:n], cnt[0], 1.0, t)
                PS.put(b, u)
                out_.append(u)
            return t, out_

        def cols(v, c, j):
            return v[:, c, 128 * j:128 * j + 128]

        def table(src, n, g):
            sl = CR.get()
            return sl, sl.buf[:, 0:n].rearrange("p (g n) -> p g n", g=g), sl.load(S, [(sl.buf[:, 0:n], src)])

        def attend(units, tbuf, pbuf, *w0):
            tfree = [[], []]
            pfree = [[], []]
            st = {}

            def scores(k):
                u = units[k]
                tb = tbuf[:, k % 2, :]
                banks, bt = [], []
                for blk in u["scores"]:
                    b = PS.get()
                    t = mm([(b[:, 256 * n:256 * n + 256], [qk]) for n, qk in enumerate(blk)], w0, b.free)
                    banks.append(b)
                    bt.append(t)
                ends = []
                for g in u["soft"]:
                    mcol, first = g["m"], True
                    for (bi, c0, n, tab, tabtok, col0) in g["parts"]:
                        src = banks[bi][:, c0:c0 + n]
                        dst = tb[:, col0:col0 + n]
                        if tab is not None:
                            if len(tab.shape) == 3:
                                src = src.rearrange("p (k n) -> p k n", k=tab.shape[1])
                                dst = dst.rearrange("p (k n) -> p k n", k=tab.shape[1])
                            t = ttr(dst, src, tab, ALU.add, ALU.max, LOW if first else mcol, mcol,
                                    bt[bi], tabtok, tfree[k % 2])
                        else:
                            t = red(mcol, src, ALU.max, bt[bi], tfree[k % 2])
                        first = False
                    if g.get("done"):
                        g["done"](t)
                    if g.get("nsink") is not None:
                        t = ts(g["nm"], mcol, -1.0, g["nsink"], ALU.mult, ALU.min, t)
                    else:
                        t = ts(g["nm"], mcol, -1.0, None, ALU.mult, None, t)
                for g in u["soft"]:
                    a0, n = g["cols"]
                    if g["parts"][0][3] is None:
                        bi, c0 = g["parts"][0][0:2]
                        t = act(tb[:, a0:a0 + n], banks[bi][:, c0:c0 + n], ACT.Exp, t, tfree[k % 2],
                                bias=g["nm"], acc=g["den"])
                    else:
                        t = act(tb[:, a0:a0 + n], tb[:, a0:a0 + n], ACT.Exp, t, bias=g["nm"], acc=g["den"])
                    ends.append(t)
                for b in banks:
                    PS.put(b, *ends)
                st[k] = ends

            def turns(k):
                nb = units[k]["nblk"]
                tb = tbuf[:, k % 2, :]
                ev = []
                for c in range(0, nb, 4):
                    m = min(4, nb - c)
                    b = PS.get()
                    t = tr([(b[:, 128 * n:128 * n + 128], tb[:, 128 * (c + n):128 * (c + n) + 128])
                            for n in range(m)], st[k], b.free)
                    E = A if (k + c // 4) % 2 else V
                    u = cp(E, pbuf[:, k % 2, 128 * c:128 * (c + m)], b[:, 0:128 * m], t, pfree[k % 2])
                    PS.put(b, u)
                    ev.append(u)
                tfree[k % 2] = [t]
                st[k] = ev

            def values(k):
                t = mm([(o, [(pbuf[:, k % 2, 128 * n:128 * n + 128], v) for n, v in prs])
                        for o, prs in units[k]["pv"]], st[k], units[k].get("ofree"))
                pfree[k % 2] = [t]
                if units[k].get("after"):
                    units[k]["after"](t)

            for k in range(len(units) + 2):
                if k < len(units):
                    scores(k)
                if 1 <= k <= len(units):
                    turns(k - 1)
                if k >= 2:
                    values(k - 2)

        def mixer(l):
            base = 0
            QK = ar[:, 0:22 * 256].rearrange("p (c t) -> p c t", c=22)
            VA = ar[:, 5632:7168].rearrange("p (i n) -> p i n", i=2)
            VW = ar[:, 7168:7680].rearrange("p (i n) -> p i n", i=2)
            GT = ar[:, 7680:11776].rearrange("p (c t) -> p c t", c=16)
            tb = ar[:, 11776:13312].rearrange("p (k n) -> p k n", k=2)
            pb = ar[:, 13312:14848].rearrange("p (k n) -> p k n", k=2)
            OA = ar[:, 14848:15360].rearrange("p (i n) -> p i n", i=2)
            OAT = ar[:, 15360:15872].rearrange("p (c t) -> p c t", c=2)
            th = norm(f"norm_mix{l}")
            W = I["w_in"][l]
            ready = []
            for j in range(3):
                tile = wload(W[:, 512 * j:512 * j + 512], 8, 512)
                t, o = proj_T(tile, cols, 4, 8, HT,
                              lambda a, m, j=j: (QK[:, 4 * j + a:4 * j + a + m, :], 0.125 if 4 * j + a < 6 else 1.0),
                              th)
                tile[0].free = [t]
                ready += o
            tile = wload(W[:, 1536:2048], 8, 512)
            t, o = proj_N(tile, 0, 512, 8, HT, lambda i: VA[:, i, 0:512], th)
            tile[0].free = [t]
            ready += o
            tile = wload(W[:, 2048:2304], 8, 256)
            t, o = proj_N(tile, 0, 256, 8, HT, lambda i: VA[:, i, 512:768], th)
            tile[0].free = [t]
            ready += o
            rd_dil = [V.last(), A.last()]

            for j in range(2):
                tile = wload(W[:, 2304 + 512 * j:2816 + 512 * j], 8, 512)
                t, o = proj_T(tile, cols, 4, 8, HT,
                              lambda a, m, j=j: (QK[:, 12 + 4 * j + a:12 + 4 * j + a + m, :], 0.125), th)
                tile[0].free = [t]
            tile = wload(W[:, 3328:3840], 8, 512)
            t, o = proj_T(tile, cols, 2, 8, HT, lambda a, m: (QK[:, 20:22, :], 1.0), th)
            t, o = proj_N(tile, 256, 256, 8, HT, lambda i: VW[:, i, :], th)
            tile[0].free = [t]
            rd_win = [V.last(), A.last()]

            def gates():
                for j in range(4):
                    tile = wload(W[:, 3840 + 512 * j:4352 + 512 * j], 8, 512)

                    def fin(a, m, b, t, j=j):
                        for k in range(m):
                            c = 4 * j + a + k
                            u = act(GT[:, c, :], b[:, 256 * k:256 * k + 256], ACT.Sigmoid, t,
                                    bias=gain(f"bgate{l}", c))
                        return u
                    t, o = proj_T(tile, cols, 4, 8, HT, lambda a, m: (None, None), th, fin)
                    tile[0].free = [t]
            gates()
            mx, nm, den = small(16, 8), small(24, 8), small(32, 8)
            units = []
            ob = [PS.get(), PS.get()]
            for s in range(4):
                got = Late(lambda s=s: table(I["cd"][s], 1152, 3))
                for i in range(2):
                    qs = slice(128 * i, 128 * i + 128)
                    off = 128 * (1 - i)
                    hs = [4 * g + s for g in range(3)]
                    qk = [(QK[64 * (h % 2):64 * (h % 2) + 64, h // 2, qs],
                           QK[64 * (h % 2):64 * (h % 2) + 64, 6 + h // 2, :]) for h in hs]
                    n = 2 * s + i
                    u = {
                        "scores": [qk[0:2], qk[2:3]],
                        "soft": [{"m": mx[:, n:n + 1], "nm": nm[:, n:n + 1], "den": den[:, n:n + 1],
                                  "parts": Late(lambda got=got, off=off: [
                                      (0, 0, 512, got[1][:, 0:2, off:off + 256], got[2], 0),
                                      (1, 0, 256, got[1][:, 2, off:off + 256], got[2], 512)]),
                                  "cols": (0, 768)}],
                        "nblk": 6,
                        "pv": [(ob[i][:, 64 * s:64 * s + 64],
                                [(2 * g + k, VA[:, k, 64 * hs[g]:64 * hs[g] + 64]) for g in range(3) for k in range(2)])],
                        "ofree": ob[i].free,
                    }
                    if i == 1:
                        u["soft"][0]["done"] = lambda t, got=got: setattr_free(got[0], t)
                    units.append(u)
            attend(units, tb, pb, rd_dil)
            t = recip(den, den, A.last(), T.last())
            dv = den.rearrange("p (s i) -> p i s", i=2)
            for i in range(2):
                t = tt(V, OA[:, i, :].rearrange("p (s d) -> p s d", s=4),
                       ob[i][:, 0:256].rearrange("p (s d) -> p s d", s=4),
                       dv[:, i, :].unsqueeze(2).to_broadcast([P, 4, 64]), ALU.mult)
                PS.put(ob[i], t)
            toa = to_T(OAT, OA, 2, None, t)

            mx, nm, den, ns, es = small(48, 32), small(80, 32), small(112, 32), small(144, 16), small(160, 32)
            ts(ns, B(f"sink{l}"), -1.0, None, ALU.mult, None)
            ob2 = {}
            OB = Y

            def flush(i, half, t):
                b = ob2.pop((i, half))
                lo = 16 * i + 8 * half
                a = tt(V, es[:, lo:lo + 8], B(f"sink{l}")[:, 8 * half:8 * half + 8], nm[:, lo:lo + 8], ALU.add, A.last())
                a = act(es[:, lo:lo + 8], es[:, lo:lo + 8], ACT.Exp, a)
                a = tt(V, den[:, lo:lo + 8], den[:, lo:lo + 8], es[:, lo:lo + 8], ALU.add, a)
                a = recip(den[:, lo:lo + 8], den[:, lo:lo + 8])
                a = tt(V, OB[:, i, 512 * half:512 * half + 512].rearrange("p (s d) -> p s d", s=8),
                       b[:, :].rearrange("p (s d) -> p s d", s=8),
                       den[:, lo:lo + 8].unsqueeze(2).to_broadcast([P, 8, 64]), ALU.mult, t)
                PS.put(b, a)

            def win_unit(i, hp, tab, tok, sl, bank):
                qs = slice(128 * i, 128 * i + 128)
                off = 128 * (1 - i)
                hs = [2 * hp, 2 * hp + 1]
                kv = hs[0] // 4
                bp = 64 * (kv % 2)
                qk = []
                for h in hs:
                    c = 12 + 4 * (h // 8) + h % 4
                    qk.append((QK[bp:bp + 64, c, qs], QK[bp:bp + 64, 20 + kv // 2, :]))
                soft = []
                for n, h in enumerate(hs):
                    x = 16 * i + h
                    soft.append({"m": mx[:, x:x + 1], "nm": nm[:, x:x + 1], "den": den[:, x:x + 1],
                                 "parts": [(0, 256 * n, 256, tab[:, h % 4, off:off + 256], tok, 256 * n)],
                                 "cols": (256 * n, 256), "nsink": ns[:, h:h + 1]})
                if hp % 2:
                    soft[1]["done"] = lambda t: setattr_free(sl, t)
                return {
                    "scores": [qk], "soft": soft, "nblk": 4,
                    "pv": [(bank[:, 64 * (h % 8):64 * (h % 8) + 64],
                            [(2 * n + k, VW[:, k, 64 * kv:64 * kv + 64]) for k in range(2)])
                           for n, h in enumerate(hs)],
                    "ofree": bank.free,
                }

            for i in range(2):
                for half in range(2):
                    bank = PS.get()
                    ob2[(i, half)] = bank
                    us = []
                    for gq in range(2 * half, 2 * half + 2):
                        sl, tab, tok = table(I["cw"][gq], 1536, 4)
                        for hp in (2 * gq, 2 * gq + 1):
                            us.append(win_unit(i, hp, tab, tok, sl, bank))
                    attend(us, tb, pb, rd_win, T.last())
                    flush(i, half, T.last())
            OBT = HT
            tob = to_T(OBT, OB, 8, None, V.last(), T.last())
            MT = Y[:, :, :].rearrange("p i (c t) -> p (i c) t", t=256)
            wa = wload(I["w_branch_a"][l], 2, 1024)
            wbs = []
            ready = [V.last(), A.last(), T.last()]
            ya_tok = []
            for j in range(0, 8, 2):
                b = PS.get()
                t = mm([(b[:, 256 * k:256 * k + 256], [(wa[1][:, c, 128 * (j + k):128 * (j + k) + 128], OAT[:, c, :])
                                                       for c in range(2)]) for k in range(2)], wa[2], ready, b.free)
                u = tt(V, MT[:, j:j + 2, :], b[:, :].rearrange("p (k t) -> p k t", k=2), GT[:, j:j + 2, :], ALU.mult, t)
                PS.put(b, u)
            wa[0].free = [t]
            for half in range(2):
                wb = wload(I["w_branch_b"][l][:, 512 * half:512 * half + 512], 8, 512)
                for j in range(0, 4, 2):
                    b = PS.get()
                    t = mm([(b[:, 256 * k:256 * k + 256], [(cols(wb[1], c, j + k), OBT[:, c, :])
                                                           for c in range(8)]) for k in range(2)], wb[2], b.free)
                    jj = 4 * half + j
                    tmp = tb[:, (j // 2) % 2, 0:512].rearrange("p (k t) -> p k t", k=2)
                    u = tt(V, tmp, b[:, :].rearrange("p (k t) -> p k t", k=2), GT[:, 8 + jj:10 + jj, :], ALU.mult, t)
                    PS.put(b, u)
                    u = tt(V, MT[:, jj:jj + 2, :], MT[:, jj:jj + 2, :], tmp, ALU.add)
                wb[0].free = [t]
            residual(MT, I["w_out"][l], u)

        def setattr_free(sl, t):
            sl.free = [t]

        def residual(MT, W, *w):
            for half in range(2):
                wo = wload(W[:, 512 * half:512 * half + 512], 8, 512)
                for i in range(2):
                    b = PS.get()
                    t = mm([(b[:, :], [(MT[:, c, 128 * i:128 * i + 128], wo[1][:, c, :]) for c in range(8)])],
                           wo[2], b.free, *w)
                    x = X[:, i, 512 * half:512 * half + 512]
                    PS.put(b, tt(V, x, x, b[:, :], ALU.add, t))
                wo[0].free = [t]

        zt = []

        def experts(l, extra):
            PA = ar[:, 0:1024].rearrange("p (i n) -> p i n", i=2)
            PG = ar[:, 1024:2048].rearrange("p (i n) -> p i n", i=2)
            PT = ar[:, 2048:3072].rearrange("p (g t) -> p g t", g=4)
            XE = ar[:, 3072:7168].rearrange("p (c n) -> p c n", c=8)
            wr = ar[:, 7168:7296].rearrange("p (c n) -> p c n", c=8)
            SI = ar[:, 7296:9344].rearrange("p (k n) -> p k n", k=2)
            AT = ar[:, 9344:11392].rearrange("p (k c n) -> p k c n", k=2, c=8)
            YE = ar[:, 11392:12416]
            af = ar[:, 12416:12448].rearrange("p (i n) -> p i n", i=2)
            mk = ar[:, 12448:12480].rearrange("p (i n) -> p i n", i=2)
            ky = ar[:, 12480:12512].rearrange("p (i n) -> p i n", i=2)
            aT = ar[0:16, 12544:12800]
            wk = [ar[0:16, 12800:13056], ar[0:16, 13056:13312]]
            mT = ar[0:16, 13312:13568]
            t8 = ar[0:16, 13568:13576]
            twr = one[2].load(S, [(wr, I["w_router"][l].rearrange("(c p) n -> p c n", p=P))], T.last(), V.last(), A.last())
            th = norm(f"norm_ffn{l}")
            m1, s1 = small(16, 2), small(18, 2)
            b = PS.get()
            for i in range(2):
                t = mm([(b[:, 16 * i:16 * i + 16], [(HT[:, c, 128 * i:128 * i + 128], wr[:, c, :]) for c in range(8)])],
                       th, twr, b.free)
            red(m1, b[:, 0:32].rearrange("p (i n) -> p i n", i=2), ALU.max, t)
            u = ts(m1, m1, -1.0, None, ALU.mult, None)
            for i in range(2):
                u = act(af[:, i, :], b[:, 16 * i:16 * i + 16], ACT.Exp, u, bias=m1[:, i:i + 1], acc=s1[:, i:i + 1])
            recip(s1, s1, u)
            for i in range(2):
                u = ts(af[:, i, :], af[:, i, :], s1[:, i:i + 1], None, ALU.mult, None)
            t = tr([(b[0:16, 128 + 128 * i:256 + 128 * i], af[:, i, :]) for i in range(2)], u)
            cp(V, aT, b[0:16, 128:384], t)
            src = aT
            for r in range(4):
                dst = wk[r % 2]
                V.op(lambda e, s=src: e.max(t8, s))
                u = V.op(lambda e, s=src, d=dst: e.match_replace(d, t8, s, -1.0))
                src = dst
            u = ts(mT, src, 0.0, None, ALU.is_lt, None)
            PS.put(b, u)
            b = PS.get()
            t = tr([(b[:, 16 * i:16 * i + 16], mT[:, 128 * i:128 * i + 128]) for i in range(2)], u, b.free)
            u = cp(V, mk, b[:, 0:32].rearrange("p (i n) -> p i n", i=2), t)
            t = mm([(b[:, 64:80], [(C("ustr"), mk[:, 0, :])]),
                    (b[:, 80:96], [(C("ones"), mk[:, 0, :]), (C("ustr"), mk[:, 1, :])])], u)
            u = stt(ky, b[:, 64:96].rearrange("p (i n) -> p i n", i=2), 1.0, mk, ALU.add, ALU.mult, t)
            PS.put(b, u)
            ts(ky, ky, 1.0, None, ALU.subtract, None)
            for i in range(2):
                pv = PA[:, i, :].rearrange("p (e c) -> p e c", e=16)
                u = tt(V, pv, C("iota").unsqueeze(1).to_broadcast([P, 16, 32]),
                       ky[:, i, :].unsqueeze(2).to_broadcast([P, 16, 32]), ALU.is_equal)
            tpa = u
            for i in range(2):
                u = tt(V, PG[:, i, :].rearrange("p (e c) -> p e c", e=16), PA[:, i, :].rearrange("p (e c) -> p e c", e=16),
                       af[:, i, :].unsqueeze(2).to_broadcast([P, 16, 32]), ALU.mult)
            tpg = u
            xe_t = []
            for c in range(8):
                b = PS.get()
                t = mm([(b[:, :], [(Y[:, i, 128 * c:128 * c + 128], PA[:, i, :]) for i in range(2)])], tpa, b.free)
                if c % 2:
                    u = ts(XE[:, c, :], b[:, :], gain(f"norm_ffn{l}", c), None, ALU.mult, None, t)
                else:
                    u = act(XE[:, c, :], b[:, :], ACT.Copy, t, scale=gain(f"norm_ffn{l}", c))
                PS.put(b, u)
                xe_t.append(u)
            for g in range(0, 4, 2):
                b = PS.get()
                t = tr([(b[:, 256 * k + 128 * i:256 * k + 128 * i + 128], PG[:, i, 128 * (g + k):128 * (g + k) + 128])
                        for k in range(2) for i in range(2)], tpg, b.free)
                u = cp(V if g else A, PT[:, g:g + 2, :], b[:, :].rearrange("p (k t) -> p k t", k=2), t)
                PS.put(b, u)
                xe_t.append(u)
            xe_t = xe_t[-4:]


            def gate_up(g):
                banks = {}
                for name, Wn in (("a", "w_expert_gate"), ("u", "w_expert_up")):
                    bs = [PS.get(), PS.get()]
                    for k in range(4):
                        e_ = 4 * g + k
                        tl = [wload(I[Wn][l, e_, 512 * h:512 * h + 512, :], 4, 1024) for h in range(2)]
                        for h in range(2):
                            def f(e, h=h, k=k, e_=e_, tl=tl, bs=bs):
                                for n in range(2):
                                    for c in range(4):
                                        m = e.matmul(bs[n][32 * k:32 * k + 32, :],
                                                     XE[:, 4 * h + c, 32 * e_:32 * e_ + 32],
                                                     tl[h][1][:, c, 512 * n:512 * n + 512],
                                                     start=(h == 0 and c == 0), stop=(h == 1 and c == 3),
                                                     tile_position=(0, 32 * k))
                                return m
                            t = T.op(f, tl[h][2], xe_t, bs[0].free, bs[1].free)
                            tl[h][0].free = [t]
                    banks[name] = (bs, t)
                ab, ta = banks["a"]
                ub, tu = banks["u"]
                s_ = SI[:, g % 2, :]
                for n in range(2):
                    u = act(s_[:, 512 * n:512 * n + 512], ab[n][:, :], ACT.Silu, ta)
                    PS.put(ab[n], u)
                for n in range(2):
                    v = tt(V, s_[:, 512 * n:512 * n + 512], s_[:, 512 * n:512 * n + 512], ub[n][:, :], ALU.mult, u, tu)
                    PS.put(ub[n], v)
                return v

            def turn(g, v):
                us = []
                for c in range(0, 8, 4):
                    b = PS.get()
                    t = tr([(b[:, 128 * k:128 * k + 128], SI[:, g % 2, 128 * (c + k):128 * (c + k) + 128])
                            for k in range(4)], v, b.free)
                    u = cp(V if c else A, AT[:, g % 2, c:c + 4, :], b[:, :].rearrange("p (k n) -> p k n", k=4), t)
                    PS.put(b, u)
                    us.append(u)
                return us

            def down(g, us):
                bs = [PS.get(), PS.get()]
                for k in range(4):
                    e_ = 4 * g + k
                    tl = [wload(I["w_expert_down"][l, e_, 512 * h:512 * h + 512, :], 4, 1024) for h in range(2)]
                    for h in range(2):
                        def f(e, h=h, k=k, tl=tl):
                            for n in range(2):
                                for c in range(4):
                                    m = e.matmul(bs[n][32 * k:32 * k + 32, :], AT[:, g % 2, 4 * h + c, 32 * k:32 * k + 32],
                                                 tl[h][1][:, c, 512 * n:512 * n + 512],
                                                 start=(h == 0 and c == 0), stop=(h == 1 and c == 3),
                                                 tile_position=(0, 32 * k))
                            return m
                        t = T.op(f, tl[h][2], us, bs[0].free, bs[1].free)
                        tl[h][0].free = [t]
                us = []
                for n in range(2):
                    u = cp(A if n else V, YE[:, 512 * n:512 * n + 512], bs[n][:, :], t)
                    PS.put(bs[n], u)
                    us.append(u)
                for i in range(2):
                    for n in range(2):
                        b = PS.get()
                        t = mm([(b[:, :], [(PT[:, g, 128 * i:128 * i + 128], YE[:, 512 * n:512 * n + 512])])], us, b.free)
                        x = X[:, i, 512 * n:512 * n + 512]
                        PS.put(b, tt(V, x, x, b[:, :], ALU.add, t))

            prev = None
            for g in range(4):
                v = gate_up(g)
                next(extra, None)
                if prev is not None:
                    down(g - 1, prev)
                prev = turn(g, v)
            down(3, prev)
            for _ in extra:
                pass

        KM = [cbuf[:, l, 0:512].rearrange("p (c t) -> p c t", c=2) for l in range(2)]
        VM = [cbuf[:, l, 512:1024].rearrange("p (i n) -> p i n", i=2) for l in range(2)]

        def rel_tables():
            oh = ar[0:32, 13824:14335]
            rb = small(480, 12)[0:32, :]
            t0 = one[3].load(S, [(oh, I["oh"]), (rb, I["rel_bias_2"])], V.last(), A.last(), T.last(), G.last())
            w = None
            for q in range(3):
                us = []
                for h in range(4):
                    b = PS.get()
                    t = mm([(b[:, 0:511], [(rb[:, 4 * q + h:4 * q + h + 1].to_broadcast([32, 128]), oh)])], t0, b.free)
                    u = cp(A if h % 2 else V, ar[:, 14336 + 512 * h:14336 + 512 * h + 511], b[:, 0:511], t, w)
                    PS.put(b, u)
                    us.append(u)
                w = one[4].load(A, [(zd[4 * q + h, :, 0:511], ar[:, 14336 + 512 * h:14336 + 512 * h + 511])
                                    for h in range(4)], us)
                yield
            zt.append(w)
            for E in (V, A):
                E.wait(w)

        def memory():
            last = [T.last(), V.last(), A.last(), G.last()]
            t = one[5].load(S, [(Y[:, :, :], I["mem_2"][0].rearrange("(i p) n -> p i n", p=P))], last)
            r = small(232, 2)
            junk = ar[:, 15360:16384]
            u = rstd([Y[:, 0, :], Y[:, 1, :]], 1024, r, [junk, junk], t)
            a = ts(Y[:, 0, :], Y[:, 0, :], r[:, 0:1], None, ALU.mult, None, u)
            b = act(Y[:, 1, :], Y[:, 1, :], ACT.Copy, u, scale=r[:, 1:2])
            th = to_T(HT, Y, 8, "mem", a, b, last)
            yield
            for l in range(2):
                tile = wload(I["w_mem_kv_2"][l], 8, 512)
                proj_T(tile, cols, 2, 8, HT, lambda a, m, l=l: (KM[l], 1.0), th)
                t, o = proj_N(tile, 256, 256, 8, HT, lambda i, l=l: VM[l][:, i, :], th)
                tile[0].free = [t]
                yield

        def bcast_row(name, dst, s, *w):
            a, b = PR[name]
            return s.load(S, [(dst, I["pr"][0:1, a:b].to_broadcast([P, b - a]))], *w)

        def row_norm(name, dst, slot):
            gb = ar[:, 15360:16384]
            tg = bcast_row(name, gb, slot, V.last(), A.last(), T.last(), G.last())
            r = small(8, 2)
            t = rstd([X[:, 0, :], X[:, 1, :]], 1024, r, [Y[:, 0, :], Y[:, 1, :]], V.last(), T.last())
            for i in range(2):
                t = stt(dst[:, i, :], X[:, i, :], r[:, i:i + 1], gb, ALU.mult, ALU.mult, t, tg, A.last())
            return t

        def mem_units(l, QM, tb, OM, ob, w):
            mx, nm, den = small(208, 8), small(216, 8), small(224, 8)
            us = []
            for i in range(2):
                for hp in range(2):
                    qs = slice(128 * i, 128 * i + 128)
                    qk, soft = [], []
                    for n in range(2):
                        h = 2 * hp + n
                        x = 4 * i + h
                        qk.append((QM[64 * n:64 * n + 64, hp, qs], KM[l][64 * n:64 * n + 64, hp, :]))
                        soft.append({"m": mx[:, x:x + 1], "nm": nm[:, x:x + 1], "den": den[:, x:x + 1],
                                     "parts": [(n, 0, 256, None, None, 256 * n)], "cols": (256 * n, 256)})
                    us.append({"scores": [qk[0:1], qk[1:2]], "soft": soft, "nblk": 4,
                               "pv": [(ob[:, 256 * i + 64 * (2 * hp + n):256 * i + 64 * (2 * hp + n) + 64],
                                       [(2 * n + k, VM[l][:, k, 64 * (2 * hp + n):64 * (2 * hp + n) + 64]) for k in range(2)])
                                      for n in range(2)], "ofree": ob.free})

            def flush():
                recip(den, den, A.last(), T.last())
                for i in range(2):
                    t = tt(V, OM[:, i, :].rearrange("p (s d) -> p s d", s=4),
                           ob[:, 256 * i:256 * i + 256].rearrange("p (s d) -> p s d", s=4),
                           den[:, 4 * i:4 * i + 4].unsqueeze(2).to_broadcast([P, 4, 64]), ALU.mult)
                PS.put(ob, t)
                return t
            return us, flush

        def mix_a(zt, tmem):
            l = 0
            QT = ar[:, 0:1536].rearrange("p (c t) -> p c t", c=6)
            KT = ar[:, 1536:3072].rearrange("p (c t) -> p c t", c=6)
            VV = ar[:, 3072:4608].rearrange("p (i n) -> p i n", i=2)
            IQ = ar[:, 4608:5632].rearrange("p (c t) -> p c t", c=4)
            IK = ar[:, 5632:5888]
            QM = ar[:, 5888:6400].rearrange("p (c t) -> p c t", c=2)
            CK = ar[:, 6400:6912].rearrange("p (i n) -> p i n", i=2)
            CT = ar[:, 6912:7424].rearrange("p (c t) -> p c t", c=2)
            BH = ar[:, 7424:12032].rearrange("p (h n) -> p h n", h=12)
            tb = ar[:, 12032:13056].rearrange("p (k n) -> p k n", k=2)
            pb = ar[:, 13056:14080].rearrange("p (k n) -> p k n", k=2)
            SC = ar[:, 14080:14592].rearrange("p (i n) -> p i n", i=2)
            RL = ar[:, 14592:15104].rearrange("p (i n) -> p i n", i=2)
            BM = ar[:, 15104:16128].rearrange("p (k n) -> p k n", k=4)
            IW = small(240, 16).rearrange("p (i n) -> p i n", i=2)
            t8 = small(256, 8)
            th = norm("mix20")
            tbh = one[6].load(S, [(BH[:, h, :], bass.AP(tensor=zd.tensor, offset=h * 65536 + 127,
                                                         ap=[[511, 128], [1, 384]])) for h in range(12)],
                              zt, T.last(), V.last(), A.last())
            W = I["a_w_in_2"][0]
            tile = wload(W[:, 0:512], 8, 512)
            t, o = proj_T(tile, cols, 4, 8, HT, lambda a, m: (QT[:, a:a + m, :], 0.125), th)
            tile[0].free = [t]
            tile = wload(W[:, 512:1024], 8, 512)
            t, o = proj_T(tile, cols, 2, 8, HT, lambda a, m: (QT[:, 4:6, :], 0.125), th)
            t, o = proj_N(tile, 256, 256, 8, HT, lambda i: CK[:, i, :], th)
            tile[0].free = [t]
            tile = wload(W[:, 1024:1536], 8, 512)
            t, o = proj_T(tile, cols, 4, 8, HT, lambda a, m: (IQ[:, a:a + m, :], 0.125), th)
            tile[0].free = [t]
            tile = wload(W[:, 1536:1864], 8, 328)
            sl, v, tw = tile
            b = PS.get()
            t = mm([(b[0:64, 0:256], [(v[:, c, 0:64], HT[:, c, :]) for c in range(8)])], tw, th, b.free)
            t = mm([(b[64:128, 0:256], [(v[:, c, 0:64], HT[:, c, :]) for c in range(8)])])
            u = cp(A, IK, b[:, 0:256], t)
            PS.put(b, u)
            b = PS.get()
            t = mm([(b[:, 8 * i:8 * i + 8], [(HT[:, c, 128 * i:128 * i + 128], v[:, c, 64:72]) for c in range(8)])
                    for i in range(2)], b.free)
            u = ts(IW, b[:, 0:16].rearrange("p (i n) -> p i n", i=2), 8.0 ** -0.5, None, ALU.mult, None, t)
            PS.put(b, u)
            t, o = proj_T(tile, lambda v, c, j: v[:, c, 72 + 128 * j:200 + 128 * j], 2, 8, HT,
                          lambda a, m: (QM, 0.125), th)
            sl.free = [t]
            r = small(8, 2)
            t = rstd([CK[:, 0, :], CK[:, 1, :]], 256, r, [SC[:, 0, :], SC[:, 1, :]], V.last())
            for i in range(2):
                t = stt(CK[:, i, :], CK[:, i, :], r[:, i:i + 1], B("kvn"), ALU.mult, ALU.mult, t, A.last())
            tct = to_T(CT, CK, 2, None, t)
            tct = [V.last(), A.last()]
            wk_ = wload(I["uk"], 2, 768)
            for j in range(0, 6, 2):
                b = PS.get()
                t = mm([(b[:, 256 * k:256 * k + 256], [(wk_[1][:, c, 128 * (j + k):128 * (j + k) + 128], CT[:, c, :])
                                                       for c in range(2)]) for k in range(2)], wk_[2], tct, b.free)
                u = cp(A, KT[:, j:j + 2, :], b[:, :].rearrange("p (k t) -> p k t", k=2), t)
                PS.put(b, u)
            wk_[0].free = [t]
            wv_ = wload(I["uv"], 2, 768)
            for i in range(2):
                for c0, n in ((0, 512), (512, 256)):
                    b = PS.get()
                    t = mm([(b[:, 0:n], [(CT[:, c, 128 * i:128 * i + 128], wv_[1][:, c, c0:c0 + n]) for c in range(2)])],
                           wv_[2], b.free)
                    u = cp(A, VV[:, i, c0:c0 + n], b[:, 0:n], t)
                    PS.put(b, u)
            wv_[0].free = [t]
            rl_free = [[], []]
            for i in range(2):
                for hp in range(4):
                    bs = [PS.get(), PS.get()]
                    t = mm([(bs[n][:, 0:256], [(IQ[64 * n:64 * n + 64, hp, 128 * i:128 * i + 128],
                                                IK[64 * n:64 * n + 64, :])]) for n in range(2)],
                           V.last() if hp == 0 else None, A.last() if hp == 0 else None, bs[0].free, bs[1].free)
                    for n in range(2):
                        h = 2 * hp + n
                        u = act(RL[:, n, :], bs[n][:, 0:256], ACT.Relu, t, rl_free[n])
                        PS.put(bs[n], u)
                        in1 = SC[:, i, :] if h else C("causal")[:, 256 * i:256 * i + 256]
                        x = stt(SC[:, i, :], RL[:, n, :], IW[:, i, h:h + 1], in1, ALU.mult, ALU.add, u)
                        rl_free[n] = [x]
            mask = []
            for i in range(2):
                src = SC[:, i, :]
                for r_ in range(8):
                    dst = RL[:, r_ % 2, :]
                    V.op(lambda e, s=src: e.max(t8, s))
                    V.op(lambda e, s=src, d=dst: e.match_replace(d, t8, s, LOW))
                    src = dst
                ts(SC[:, i, :], src, -2.0e38, NEG, ALU.is_ge, ALU.mult)
                mask.append(tt(V, SC[:, i, :], SC[:, i, :], C("causal")[:, 256 * i:256 * i + 256], ALU.add))
            mx, nm, den = small(16, 24), small(40, 24), small(64, 24)
            OS = Y[:, :, 0:768]
            OM = Y[:, :, 768:1024]
            bmfree = [[] for _ in range(4)]
            nb = [0]
            ops = {}
            ob = PS.get()
            mu, mflush = mem_units(l, QM, tb, OM, ob, tmem)
            attend(mu, tb, pb, V.last(), A.last(), tmem)
            mflush()
            for i in range(2):
                obs = [PS.get(), PS.get()]
                us = []
                for hp in range(6):
                    qs = slice(128 * i, 128 * i + 128)
                    off = 128 * (1 - i)
                    qk, soft = [], []
                    for n in range(2):
                        h = 2 * hp + n
                        x = 12 * i + h
                        s_ = nb[0] % 4
                        nb[0] += 1
                        tbm = [None]
                        qk.append((QT[64 * n:64 * n + 64, hp, qs], KT[64 * n:64 * n + 64, hp, :]))
                        soft.append({"m": mx[:, x:x + 1], "nm": nm[:, x:x + 1], "den": den[:, x:x + 1],
                                     "mk": (s_, h, i, off), "cols": (256 * n, 256)})
                    us.append({"scores": [qk[0:1], qk[1:2]], "soft": soft, "nblk": 4,
                               "pv": [(obs[h // 8][:, 64 * (h % 8):64 * (h % 8) + 64],
                                       [(2 * n + k, VV[:, k, 64 * h:64 * h + 64]) for k in range(2)])
                                      for n, h in ((0, 2 * hp), (1, 2 * hp + 1))],
                               "ofree": [obs[0].free, obs[1].free]})
                for u_ in us:
                    for n, g in enumerate(u_["soft"]):
                        s_, h, i_, off_ = g["mk"]
                        g["parts"] = Late(lambda s_=s_, h=h, i_=i_, off_=off_, n=n: [(
                            n, 0, 256, BM[:, s_, :],
                            tt(G, BM[:, s_, :], BH[:, h, off_:off_ + 256], SC[:, i_, :], ALU.add, tbh, mask[i_], bmfree[s_]),
                            256 * n)])
                        g["done"] = lambda t, s_=s_: bmfree.__setitem__(s_, [t])
                attend(us, tb, pb, V.last(), A.last())
                recip(den[:, 12 * i:12 * i + 12], den[:, 12 * i:12 * i + 12], A.last(), T.last())
                for b_, (h0, nh) in zip(obs, ((0, 8), (8, 4))):
                    t = tt(V, OS[:, i, 64 * h0:64 * (h0 + nh)].rearrange("p (s d) -> p s d", s=nh),
                           b_[:, 0:64 * nh].rearrange("p (s d) -> p s d", s=nh),
                           den[:, 12 * i + h0:12 * i + h0 + nh].unsqueeze(2).to_broadcast([P, nh, 64]), ALU.mult)
                    PS.put(b_, t)
            to_T(HT, Y, 8, None, V.last(), T.last())
            residual(HT, I["w_o_2"][0], V.last(), A.last())

        def mix_b():
            l = 1
            ZT = ar[:, 0:1536].rearrange("p (i n) -> p i n", i=2)
            XR = ar[:, 1536:4126].rearrange("p (c t) -> p c t", c=10)
            XC = ar[:, 4126:6686].rearrange("p (c t) -> p c t", c=10)
            XS = ar[:, 6686:8222].rearrange("p (i n) -> p i n", i=2)
            XD = ar[:, 8222:9758].rearrange("p (i n) -> p i n", i=2)
            QM = ar[:, 9758:10270].rearrange("p (c t) -> p c t", c=2)
            CB = ar[:, 10270:11038].rearrange("p (g n) -> p g n", g=2)
            EE = ar[:, 11038:11806].rearrange("p (k n) -> p k n", k=2)
            tb = ar[:, 11806:12830].rearrange("p (k n) -> p k n", k=2)
            pb = ar[:, 12830:13854].rearrange("p (k n) -> p k n", k=2)
            TM = ar[:, 13854:14366].rearrange("p (k n) -> p k n", k=2)
            TR = ar[:, 14366:15902].rearrange("p (i n) -> p i n", i=2)
            dt, da, nac, ea = (small(256 + 24 * k, 24).rearrange("p (i n) -> p i n", i=2) for k in range(4))
            u1, u2 = small(352, 24).rearrange("p (i n) -> p i n", i=2), small(376, 24).rearrange("p (i n) -> p i n", i=2)
            ng = small(400, 12)
            eb = small(412, 12)
            th = norm("mix21")
            W = I["b_w_in_2"][0]
            V.op(lambda e: e.memset(XR[:, :, 0:3], 0.0))
            tile = wload(W[:, 0:512], 8, 512)
            t, o = proj_N(tile, 0, 512, 8, HT, lambda i: ZT[:, i, 0:512], th)
            tile[0].free = [t]
            tile = wload(W[:, 512:768], 8, 256)
            t, o = proj_N(tile, 0, 256, 8, HT, lambda i: ZT[:, i, 512:768], th)
            tile[0].free = [t]
            for j, n in ((0, 4), (4, 4), (8, 2)):
                tile = wload(W[:, 768 + 128 * j:768 + 128 * (j + n)], 8, 128 * n)
                t, o = proj_T(tile, cols, n, 8, HT, lambda a, m, j=j: (XR[:, j + a:j + a + m, 3:259], 1.0), th)
                tile[0].free = [t]
            tile = wload(W[:, 2048:2316], 8, 268)
            sl, v, tw = tile
            b = PS.get()
            t = mm([(b[:, 12 * i:12 * i + 12], [(HT[:, c, 128 * i:128 * i + 128], v[:, c, 0:12]) for c in range(8)])
                    for i in range(2)], tw, b.free)
            t = tt(V, u1, b[:, 0:24].rearrange("p (i n) -> p i n", i=2),
                   B("dtb").unsqueeze(1).to_broadcast([P, 2, 12]), ALU.add, t)
            PS.put(b, t)
            t, o = proj_T(tile, lambda v, c, j: v[:, c, 12 + 128 * j:140 + 128 * j], 2, 8, HT,
                          lambda a, m: (QM, 0.125), th)
            sl.free = [t]
            ts(u2, u1, -1.0, None, ALU.mult, None)
            t = tt(V, u2, u2, u1, ALU.min)
            t = act(u2, u2, ACT.Exp, t)
            t = act(u2, u2, ACT.Ln, bias=1.0)
            t2 = act(ng, B("alog"), ACT.Exp)
            t = stt(dt, u1, 0.0, u2, ALU.max, ALU.add, t2)
            t = ts(ng, ng, -1.0, None, ALU.mult, None, t2)
            t = tt(V, da, dt, ng.unsqueeze(1).to_broadcast([P, 2, 12]), ALU.mult)
            b = PS.get()
            t = mm([(b[:, 0:24], [(C("uinc"), small(280, 24))]),
                    (b[:, 24:36], [(C("ones"), da[:, 0, :])])], t, b.free)
            ts(nac, b[:, 0:24].rearrange("p (i n) -> p i n", i=2), -1.0, None, ALU.mult, None, t)
            t = tt(V, eb, b[:, 24:36], nac[:, 0, :], ALU.add)
            PS.put(b, t)
            k0 = PF["conv"][0]
            for c in range(10):
                def w_(k, c=c):
                    return pf[:, k0 + 10 * k + c:k0 + 10 * k + c + 1]
                ts(XC[:, c, :], XR[:, c, 0:256], w_(0), gain("convb", c), ALU.mult, ALU.add, A.last())
                for k in range(1, 4):
                    t = stt(XC[:, c, :], XR[:, c, k:k + 256], w_(k), XC[:, c, :], ALU.mult, ALU.add)
            t = act(XC[:, :, :], XC[:, :, :], ACT.Silu, t)
            t_z = act(ZT[:, :, :], ZT[:, :, :], ACT.Silu, V.last())
            for c in range(0, 6, 2):
                b = PS.get()
                u = tr([(b[:, 256 * i + 128 * k:256 * i + 128 * k + 128], XC[:, c + k, 128 * i:128 * i + 128])
                        for k in range(2) for i in range(2)], t, b.free)
                x = cp(V, XS[:, :, 128 * c:128 * c + 256], b[:, :].rearrange("p (i n) -> p i n", i=2), u)
                PS.put(b, x)
            for i in range(2):
                xd = tt(V, XD[:, i, :].rearrange("p (s d) -> p s d", s=12), XS[:, i, :].rearrange("p (s d) -> p s d", s=12),
                        dt[:, i, :].unsqueeze(2).to_broadcast([P, 12, 64]), ALU.mult)
            for g in range(2):
                b = PS.get()
                u = mm([(b[:, 0:256], [(XC[:, 6 + g, 0:128], XC[:, 8 + g, :])]),
                        (b[:, 256:384], [(XC[:, 6 + g, 128:256], XC[:, 8 + g, 128:256])])], b.free)
                x = cp(V, CB[:, g, :], b[:, 0:384], u)
                PS.put(b, x)
            OM = Y[:, :, 768:1024]
            ob = PS.get()
            mu, mflush = mem_units(l, QM, tb, OM, ob, None)
            attend(mu, tb, pb, V.last(), A.last())
            mflush()
            yb = [[PS.get(), PS.get()] for _ in range(2)]
            efree = [[], []]
            for h in range(12):
                b = PS.get()
                u = mm([(b[:, 128 * i:128 * i + 128], [(da[:, i, h:h + 1].to_broadcast([P, 128]), C("uinc"))])
                        for i in range(2)], b.free, x, xd)
                k = h % 2
                x1 = tt(V, TM[:, k, :].rearrange("p (i n) -> p i n", i=2), b[:, 0:256].rearrange("p (i n) -> p i n", i=2),
                        C("mt").unsqueeze(1).to_broadcast([P, 2, 128]), ALU.add, u, A.last())
                act(EE[:, k, 128:256], b[:, 128:256], ACT.Exp, x1, efree[k], bias=eb[:, h:h + 1])
                act(EE[:, k, 0:128], TM[:, k, 0:128], ACT.Exp, x1, bias=nac[:, 0, h:h + 1])
                x2 = act(EE[:, k, 256:384], TM[:, k, 128:256], ACT.Exp, bias=nac[:, 1, h:h + 1])
                PS.put(b, x1, x2)
                x3 = tt(V, EE[:, k, :], EE[:, k, :], CB[:, h // 6, :], ALU.mult, x2)
                hb, hc = h // 8, 64 * (h % 8)
                u = mm([(yb[0][hb][:, hc:hc + 64], [(EE[:, k, 0:128], XD[:, 0, 64 * h:64 * h + 64])]),
                        (yb[1][hb][:, hc:hc + 64], [(EE[:, k, 128:256], XD[:, 0, 64 * h:64 * h + 64]),
                                                    (EE[:, k, 256:384], XD[:, 1, 64 * h:64 * h + 64])])],
                       x3, [yb[i][j].free for i in range(2) for j in range(2)])
                efree[k] = [u]
            OS = Y[:, :, 0:768]
            for i in range(2):
                tt(V, TR[:, i, :].rearrange("p (s d) -> p s d", s=12), XS[:, i, :].rearrange("p (s d) -> p s d", s=12),
                   B("dskip").unsqueeze(2).to_broadcast([P, 12, 64]), ALU.mult)
                for j, n in ((0, 512), (1, 256)):
                    x = tt(V, TR[:, i, 512 * j:512 * j + n], TR[:, i, 512 * j:512 * j + n], yb[i][j][:, 0:n], ALU.add, u)
                    PS.put(yb[i][j], x)
                x = tt(V, TR[:, i, :], TR[:, i, :], ZT[:, i, :], ALU.mult, t_z)
            r = small(8, 2)
            t = rstd([TR[:, 0, :], TR[:, 1, :]], 768, r, [OS[:, 0, :], OS[:, 1, :]], x, T.last())
            for i in range(2):
                t = ts(OS[:, i, :], TR[:, i, :], r[:, i:i + 1], None, ALU.mult, None, t, A.last())
            to_T(HT, Y, 6, "outn", t, T.last())
            to_T(HT[:, 6:8, :], OM, 2, None)
            residual(HT, I["w_o_2"][1], V.last(), A.last())

        def peer(l):
            QT = ar[:, 0:4096].rearrange("p (c t) -> p c t", c=16)
            KS = ar[:, 4096:4352].rearrange("p (i n) -> p i n", i=2)
            SS = ar[:, 4352:4864].rearrange("p (c n) -> p c n", c=4)
            CA = ar[:, 4864:5376].rearrange("p (h n) -> p h n", h=2)
            EQ = ar[:, 5376:5888]
            R2 = ar[:, 5888:6144]
            TS = ar[:, 6144:6208].rearrange("p (c n) -> p c n", c=4)
            TIU = arU[:, 6208:6272].rearrange("p (c n) -> p c n", c=4)
            TIF = ar[:, 6272:6336].rearrange("p (c n) -> p c n", c=4)
            BS = ar[:, 6336:6368].rearrange("p (h n) -> p h n", h=2)
            PO = arU[:, 6368:6400].rearrange("p (h n) -> p h n", h=2)
            PQ = arU[:, 6400:6464].rearrange("p (s h n) -> p s h n", s=2, h=2)
            PF_ = ar[:, 6464:6528].rearrange("p (s h n) -> p s h n", s=2, h=2)
            I12 = ar[:, 6528:6592].rearrange("p (s h n) -> p s h n", s=2, h=2)
            GA = ar[:, 6656:6912].rearrange("p (i n) -> p i n", i=2)
            IX = arU[:, 6912:7168].rearrange("p (i n) -> p i n", i=2)
            DT = ar[:, 7168:7424].rearrange("p (i n) -> p i n", i=2)
            DG = ar[:, 7424:7936].rearrange("p (k n) -> p k n", k=4)
            JK = ar[:, 14336:15360]
            sums = small(16, 2)
            gb = ar[:, 15360:16384]
            last = [T.last(), V.last(), A.last(), G.last()]
            tks = one[7].load(S, [(KS, I["sk"][l])], *last)
            tg = bcast_row(f"ffn2{l}", gb, one[8], *last)
            th = norm(f"ffn2{l}")
            ty = [tt(V, Y[:, i, :], Y[:, i, :], gb, ALU.mult, tg, A.last(), T.last()) for i in range(2)]
            tq = {}

            def queries(j):
                tile = wload(I["peer_w_q_2"][l][:, 512 * j:512 * j + 512], 8, 512)
                t, tq[j] = proj_T(tile, cols, 4, 8, HT, lambda a, m, j=j: (QT[:, 4 * j + a:4 * j + a + m, :], 1.0), th)
                tile[0].free = [t]

            done_ix = {}

            def top16(tsv, tiv, src, scratch, w=None):
                V.op(lambda e: e.max(tsv[:, 0:8], src), w)
                V.op(lambda e: e.max_index(tiv[:, 0:8], tsv[:, 0:8], src))
                V.op(lambda e: e.match_replace(scratch, tsv[:, 0:8], src, LOW))
                V.op(lambda e: e.max(tsv[:, 8:16], scratch))
                return V.op(lambda e: e.max_index(tiv[:, 8:16], tsv[:, 8:16], scratch))

            def route(i, q):
                b = PS.get()
                t = mm([(b[:, 128 * k:128 * k + 128], [(QT[:, 4 * q + k, 128 * i:128 * i + 128], KS[:, k % 2, :])])
                        for k in range(4)], tq[q], tks, b.free)
                u = cp(A, SS, b[:, :].rearrange("p (k n) -> p k n", k=4), t, V.last())
                PS.put(b, u)
                yield
                for c in range(4):
                    top16(TS[:, c, :], TIU[:, c, :], SS[:, c, :], R2[:, 0:128], u)
                    yield
                cp(V, TIF, TIU)
                t4 = TS.rearrange("p (h i) n -> p h i n", i=2)
                tt(V, CA.rearrange("p h (a b) -> p h a b", a=16), t4[:, :, 0, :].unsqueeze(3).to_broadcast([P, 2, 16, 16]),
                   t4[:, :, 1, :].unsqueeze(2).to_broadcast([P, 2, 16, 16]), ALU.add)
                yield
                for h in range(2):
                    top16(BS[:, h, :], PO[:, h, :], CA[:, h, :], R2[:, 0:256])
                    yield
                gi = GA[:, i, 32 * q:32 * q + 32].rearrange("p (h n) -> p h n", h=2)
                t = tt(V, gi, BS, BS[:, :, 0:1].to_broadcast([P, 2, 16]), ALU.subtract)
                t = act(gi, gi, ACT.Exp, t)
                ts(PQ[:, 0], PO, 4, None, ALU.logical_shift_right, None)
                ts(PQ[:, 1], PO, 15, None, ALU.bitwise_and, None)
                cp(V, PF_, PQ)
                yield
                f4 = TIF.rearrange("p (h i) n -> p h i n", i=2)
                io = C("iota")[:, 0:16].unsqueeze(1).unsqueeze(1).to_broadcast([P, 2, 16, 16])
                e4 = EQ.rearrange("p (h k a) -> p h k a", h=2, k=16)
                for n in range(2):
                    tt(V, e4, PF_[:, n].unsqueeze(3).to_broadcast([P, 2, 16, 16]), io, ALU.is_equal)
                    tt(V, e4, e4, f4[:, :, n, :].unsqueeze(2).to_broadcast([P, 2, 16, 16]), ALU.mult)
                    red(I12[:, n], e4, ALU.add)
                    yield
                stt(I12[:, 0], I12[:, 0], 128.0, I12[:, 1], ALU.mult, ALU.add)
                done_ix[(i, q)] = ts(IX[:, i, 32 * q:32 * q + 32].rearrange("p (h n) -> p h n", h=2), I12[:, 0],
                                     float(l * 16384), None, ALU.add, None)
                red(sums, gi, ALU.add, t)
                recip(sums, sums)
                tt(V, gi, gi, sums.unsqueeze(2).to_broadcast([P, 2, 16]), ALU.mult)
                yield

            queries(0)
            for _ in route(0, 0):
                pass
            for j in range(1, 4):
                queries(j)
            dgfree = [[] for _ in range(4)]
            rows = (I["pu"], I["pv"])
            order = [(i, q) for i in range(2) for q in range(4)]
            acc = None
            for k_, (i, q) in enumerate(order):
                nxt = route(*order[k_ + 1]) if k_ + 1 < len(order) else iter(())
                if q == 0:
                    acc = [PS.get(), PS.get()]
                for jb in range(16 * q, 16 * q + 16):
                    sl = WR.get()
                    G.wait(sl.free, done_ix[(i, q)])
                    bufs = sl.buf.rearrange("p (k n) -> p k n", k=4)
                    for k in range(4):
                        def f(e, k=k, jb=jb, bufs=bufs, sl=sl, i=i):
                            e.indirect_dma_start(
                                out=bufs[:, k, :], out_offset=None, in_=rows[k // 2],
                                in_offset=bass.IndirectOffsetOnAxis(ap=IX[:, i, 2 * jb + k % 2:2 * jb + k % 2 + 1], axis=0),
                            ).then_inc(sl.gsem, 16)
                        G.items.append(f)
                    sl.gcnt += 64
                    tok = (sl.gsem, sl.gcnt)
                    for k in range(2):
                        j = 2 * jb + k
                        t = ttr(JK, bufs[:, k, :], Y[:, i, :], ALU.mult, ALU.add, 0.0, DT[:, i, j:j + 1], tok)
                    t = act(DT[:, i, 2 * jb:2 * jb + 2], DT[:, i, 2 * jb:2 * jb + 2], ACT.Gelu, t)
                    next(nxt, None)
                    for k in range(2):
                        j = 2 * jb + k
                        d = DG[:, j % 4, :]
                        u = ts(d, ident, DT[:, i, j:j + 1], GA[:, i, j:j + 1], ALU.mult, ALU.mult, t, dgfree[j % 4])

                        def g(e, j=j, d=d, k=k, bufs=bufs, acc=acc):
                            for n in range(2):
                                m = e.matmul(acc[n][:, :], d, bufs[:, 2 + k, 512 * n:512 * n + 512],
                                             start=(j == 0), stop=(j == 127))
                            return m
                        x = T.op(g, u, tok, acc[0].free, acc[1].free)
                        dgfree[j % 4] = [x]
                    sl.free = [x]
                for _ in nxt:
                    pass
                if q == 3:
                    for n in range(2):
                        xs = X[:, i, 512 * n:512 * n + 512]
                        PS.put(acc[n], tt(V, xs, xs, acc[n][:, :], ALU.add, x))


        for l in range(2):
            mixer(l)
            experts(l, memory() if l else rel_tables())
        row_norm("final", X, one[9])
        mix_a(zt, [V.last(), A.last()])
        peer(0)
        mix_b()
        peer(1)
        tf = row_norm("final2", Y, one[11])
        S.wait(tf, V.last())
        for i in range(2):
            S.items.append(lambda e, i=i: e.dma_start(out[0, 128 * i:128 * i + 128, :], Y[:, i, :]).then_inc(s_out, 16))
        S.items.append(lambda e: e.wait_ge(s_out, 32))

        block = ctx.enter_context(nc.Block())

        @block.sync
        def _(e):
            S.play(e)

        @block.gpsimd
        def _(e):
            G.play(e)

        @block.scalar
        def _(e):
            A.play(e)

        @block.vector
        def _(e):
            V.play(e)

        @block.tensor
        def _(e):
            T.play(e)


def _constants():
    import numpy as np
    f = np.float32
    p = np.arange(128)[:, None]
    dist = p - np.arange(384)[None, :] + 128
    ad = np.abs(dist).astype(f)

    def slopes(n):
        return (2.0 ** (-8.0 * np.arange(1, n + 1) / n)).astype(f)

    masks = [ad <= 64, dist % 4 == 0, dist % 16 == 0]
    sd, sw = slopes(12), slopes(16)
    cd = np.zeros((4, 128, 3, 384), f)
    for s in range(4):
        for g in range(3):
            cd[s, :, g] = np.where(masks[g], -sd[4 * g + s] * ad, f(NEG))
    cw = np.zeros((4, 128, 4, 384), f)
    for h in range(16):
        cw[h // 4, :, h % 4] = np.where(ad <= 128, -sw[h] * ad, f(NEG))
    n = np.maximum(255 - np.arange(511), 0)
    nf = np.maximum(n, 16).astype(f)
    large = 16 + (np.log(nf / 16) / f(np.log(8.0)) * 16).astype(np.int32)
    bucket = np.where(n < 16, n, np.minimum(large, 31))
    oh = (bucket[None, :] == np.arange(32)[:, None]).astype(f)
    co = np.zeros((128, CO["all"][1]), f)

    def put(name, a):
        co[:, CO[name][0]:CO[name][1]] = a

    q = np.arange(128)[None, :]
    put("ident", p == q)
    put("uinc", p <= q)
    put("ustr", p < q)
    put("ones", 1.0)
    k = np.arange(256)[None, :]
    put("causal", np.concatenate([np.where(k <= p + 128 * i, 0.0, NEG) for i in range(2)], axis=1))
    put("mt", np.where(p <= q, 0.0, NEG))
    put("iota", np.arange(32)[None, :])
    put("nhalf", -0.5)
    return {"cd": cd.reshape(4, 128, 1152), "cw": cw.reshape(4, 128, 1536), "oh": oh, "co": co}


def _arrays(inputs):
    import numpy as np
    g = {k: np.asarray(v) for k, v in inputs.items()}
    a = {k: np.ascontiguousarray(g[k]) for k in (
        "x", "w_branch_a", "w_branch_b", "w_out", "w_router", "w_expert_gate", "w_expert_up", "w_expert_down",
        "mem_2", "rel_bias_2", "w_o_2", "w_mem_kv_2", "a_w_in_2", "b_w_in_2", "peer_w_q_2")}
    a.update(_constants())
    w = g["w_in"]
    qw = w[:, :, 2304:3328].reshape(2, 1024, 2, 2, 4, 64).transpose(0, 1, 2, 4, 3, 5).reshape(2, 1024, 1024)
    a["w_in"] = np.ascontiguousarray(np.concatenate([w[:, :, :2304], qw, w[:, :, 3328:]], axis=2))

    def col(v):
        return v.reshape(-1, 128).T

    pf = [col(g["norm_mix"][0]), col(g["norm_mix"][1]), col(g["norm_ffn"][0]), col(g["norm_ffn"][1]),
          col(g["mix_norm_2"][0]), col(g["mix_norm_2"][1]), col(g["ffn_norm_2"][0]), col(g["ffn_norm_2"][1]),
          col(g["mem_norm_2"]), col(g["b_gate"][0]), col(g["b_gate"][1])]
    pf += [col(g["b_conv_w_2"][0, k]) for k in range(4)]
    pf += [col(g["b_conv_b_2"][0]), col(g["a_kv_norm_2"][0]), col(g["b_out_norm_2"][0])]
    a["pf"] = np.ascontiguousarray(np.concatenate(pf, axis=1))
    pr = [g["norm_final"], g["final_norm_2"], g["ffn_norm_2"][0], g["ffn_norm_2"][1], g["a_kv_norm_2"][0],
          g["sink_logit"][0], g["sink_logit"][1], g["b_dt_bias_2"][0], g["b_a_log_2"][0], g["b_d_skip_2"][0]]
    pr = np.concatenate(pr)
    a["pr"] = np.ascontiguousarray(pr.reshape(1, -1))
    a["uk"] = np.ascontiguousarray(g["a_w_uk_2"][0].transpose(1, 0, 2).reshape(256, 768))
    a["uv"] = np.ascontiguousarray(g["a_w_uv_2"][0].transpose(1, 0, 2).reshape(256, 768))
    a["sk"] = np.ascontiguousarray(g["peer_sub_keys_2"].transpose(0, 3, 1, 2))
    a["pu"] = np.ascontiguousarray(g["peer_u_2"]).reshape(32768, 1024)
    a["pv"] = np.ascontiguousarray(g["peer_v_2"]).reshape(32768, 1024)
    return a


def kernel(**inputs):
    import numpy as np
    import concourse.bacc as bacc
    from concourse.bass_utils import run_bass_kernel_spmd

    nc = bacc.Bacc("TRN2", target_bir_lowering=False, num_devices=1)
    arrays, I = {}, {}
    for name, v in _arrays(inputs).items():
        arrays[f"in_{name}"] = v
        I[name] = nc.dram_tensor(f"in_{name}", v.shape, mybir.dt.from_np(v.dtype), kind="ExternalInput").ap()
    out = nc.dram_tensor("out_0", (1, 256, 1024), F32, kind="ExternalOutput").ap()
    program(nc, I, out)
    r = run_bass_kernel_spmd(nc, [arrays], core_ids=[0])
    return r.results[0]["out_0"]
```

```python
from contextlib import ExitStack

import concourse.bass as bass
from concourse import mybir

F32 = mybir.dt.float32
U32 = mybir.dt.uint32
R32 = mybir.dt.float32r
ALU = mybir.AluOpType
ACT = mybir.ActivationFunctionType
AX_X = mybir.AxisListType.X
P = 128
NEG = -1.0e30
LOW = -3.0e38

PF = {}
PR = {}
CO = {}


def _layout():
    at = 0
    for name, n in (("norm_mix0", 8), ("norm_mix1", 8), ("norm_ffn0", 8), ("norm_ffn1", 8),
                    ("mix20", 8), ("mix21", 8), ("ffn20", 8), ("ffn21", 8), ("mem", 8),
                    ("bgate0", 16), ("bgate1", 16), ("conv", 40), ("convb", 10), ("kvn", 2), ("outn", 6)):
        PF[name] = (at, at + n)
        at += n
    PF["all"] = (0, at)
    at = 0
    for name, n in (("final", 1024), ("final2", 1024), ("ffn20", 1024), ("ffn21", 1024), ("kvn", 256),
                    ("sink0", 16), ("sink1", 16), ("dtb", 12), ("alog", 12), ("dskip", 12)):
        PR[name] = (at, at + n)
        at += n
    PR["all"] = (0, at)
    at = 0
    for name, n in (("ident", 128), ("uinc", 128), ("ustr", 128), ("ones", 128), ("causal", 512), ("mt", 128),
                    ("iota", 32), ("nhalf", 2)):
        CO[name] = (at, at + n)
        at += n
    CO["all"] = (0, at)


_layout()


class Queue:

    def __init__(self, sem):
        self.sem, self.n, self.items, self.seen = sem, 0, [], {}

    def wait(self, *toks):
        for t in toks:
            if t is None:
                continue
            if not (len(t) == 2 and isinstance(t[1], int)):
                self.wait(*t)
                continue
            sem, v = t
            if v > self.seen.get(id(sem), 0):
                self.seen[id(sem)] = v
                self.items.append(lambda e, sem=sem, v=v: e.wait_ge(sem, v))

    def last(self):
        return (self.sem, self.n) if self.n else None

    def op(self, fn, *toks):
        self.wait(*toks)
        self.n += 1
        self.items.append(lambda e, sem=self.sem: fn(e).then_inc(sem, 1))
        return (self.sem, self.n)

    def play(self, e):
        for it in self.items:
            it(e)


class Serial(Queue):

    def op(self, fn, *toks):
        return Queue.op(self, fn, self.last(), *toks)


class Slot:

    def __init__(self, buf, sem, gsem=None):
        self.buf, self.sem, self.cnt, self.free = buf, sem, 0, []
        self.gsem, self.gcnt = gsem, 0

    def load(self, q, pairs, *toks):
        q.wait(self.free, *toks)
        for dst, src in pairs:
            q.items.append(lambda e, dst=dst, src=src: e.dma_start(dst, src).then_inc(self.sem, 16))
        self.cnt += 16 * len(pairs)
        self.free = []
        return (self.sem, self.cnt)


class Late:
    def __init__(self, f):
        self.f, self.v = f, None

    def get(self):
        if self.v is None:
            self.v = self.f()
        return self.v

    def __iter__(self):
        return iter(self.get())

    def __getitem__(self, k):
        return self.get()[k]


class Two:

    def __init__(self, *slots):
        self.slots = slots

    @property
    def free(self):
        return self.slots[0].free

    @free.setter
    def free(self, toks):
        for s in self.slots:
            s.free = toks


class Ring:
    def __init__(self, slots):
        self.slots, self.n = slots, 0

    def get(self):
        self.n += 1
        s = self.slots[(self.n - 1) % len(self.slots)]
        assert s.cnt + s.gcnt == 0 or s.free
        return s


class Banks:
    def __init__(self, bufs):
        self.idle = [Bank(b) for b in bufs]

    def get(self):
        return self.idle.pop(0)

    def put(self, b, *toks):
        b.free = list(toks)
        self.idle.append(b)


class Bank:
    def __init__(self, buf):
        self.buf, self.free = buf, []

    def __getitem__(self, k):
        return self.buf[k]


def program(nc, I, out):
    ctx = ExitStack()
    with ctx:
        def sb(name, shape, dt=F32):
            return ctx.enter_context(nc.sbuf_tensor(name, shape, dt))

        def sem(name):
            return ctx.enter_context(nc.semaphore(name))

        with nc.sbuf_tensor("Y", [P, 2, 1024], F32) as Y, nc.sbuf_tensor("HT", [P, 8, 256], F32) as HT, \
                nc.sbuf_tensor("wbuf", [P, 6, 4096], F32) as wbuf:
            pass
        YR = sb("YR", [P, 8, 256], R32)
        HR = sb("HR", [P, 8, 256], R32)
        wrb = sb("wrb", [P, 6, 4096], R32)
        co = sb("co", [P, CO["all"][1]])
        pf = sb("pf", [P, PF["all"][1]])
        X = sb("X", [P, 2, 1024])
        sm = sb("sm", [P, 512])
        cbuf = sb("cbuf", [P, 2, 1536])
        ar = sb("ar", [P, 16384])
        bc = sb("bc", [P, 324])
        arU = ar[:, :].bitcast(U32)
        PS = Banks([ctx.enter_context(nc.psum_tensor(f"ps{i}", [P, 512], F32)) for i in range(8)])
        zd = nc.dram_tensor("zd", (12, 128, 512), F32, kind="Internal").ap()

        V, A, G, T = Serial(sem("sV")), Serial(sem("sA")), Serial(sem("sG")), Queue(sem("sT"))
        S = Queue(sem("sS"))
        WR = Ring([Slot(wbuf[:, k, :], sem(f"w{k}"), sem(f"g{k}")) for k in range(6)])
        for k in range(6):
            WR.slots[k].rbuf = wrb[:, k, :]
        CR = Ring([Slot(cbuf[:, k, :], sem(f"c{k}")) for k in range(2)])
        one = [Slot(None, sem(f"m{k}")) for k in range(12)]
        s_out = sem("s_out")

        def C(name):
            return co[:, CO[name][0]:CO[name][1]]

        ident = C("ident")

        def gain(name, c):
            return pf[:, PF[name][0] + c:PF[name][0] + c + 1]

        def cp(E, o, i, *w):
            if E is A:
                return E.op(lambda e: e.copy(o, i), *w)
            return E.op(lambda e: e.tensor_copy(o, i), *w)

        def tt(E, o, a, b, op, *w):
            return E.op(lambda e: e.tensor_tensor(o, a, b, op), *w)

        def ts(o, i, s1, s2, op0, op1, *w):
            if op1 is None:
                return V.op(lambda e: e.tensor_scalar(o, i, s1, None, op0), *w)
            return V.op(lambda e: e.tensor_scalar(o, i, s1, s2, op0, op1), *w)

        def stt(o, i, s, i1, op0, op1, *w):
            return V.op(lambda e: e.scalar_tensor_tensor(out=o, in0=i, scalar=s, in1=i1, op0=op0, op1=op1), *w)

        def ttr(o, a, b, op0, op1, init, acc, *w):
            return V.op(lambda e: e.tensor_tensor_reduce(o, a, b, 1.0, init, op0, op1, acc), *w)

        def act(o, i, f, *w, bias=None, scale=None, acc=None):
            kw = {}
            if bias is not None:
                kw["bias"] = bias
            if scale is not None:
                kw["scale"] = scale
            if acc is not None:
                kw["accum_out"] = acc
            return A.op(lambda e: e.activation(o, i, f, **kw), *w)

        def red(o, i, op, *w):
            return V.op(lambda e: e.tensor_reduce(o, i, AX_X, op), *w)

        def recip(o, i, *w):
            return V.op(lambda e: e.reciprocal(o, i), *w)

        def mm(groups, *w):
            def f(e):
                for o, pairs in groups:
                    for n, (l, r) in enumerate(pairs):
                        m = e.matmul(o, l, r, start=(n == 0), stop=(n == len(pairs) - 1))
                return m
            return T.op(f, *w)

        def tr(jobs, *w):
            def f(e):
                for o, i in jobs:
                    m = e.transpose(o, i, ident[0:i.shape[0], 0:i.shape[0]])
                return m
            return T.op(f, *w)

        def small(a, n):
            return sm[:, a:a + n]

        t_co = one[0].load(S, [(co[:, :], I["co"]), (pf[:, :], I["pf"]),
                               (bc[:, :], I["pr"][0:1, PR["kvn"][0]:PR["all"][1]].to_broadcast([P, 324]))])
        for i in range(2):
            t_x = one[1].load(S, [(X[:, i, :], I["x"][0, 128 * i:128 * i + 128, :])])
        for E in (V, A, G, T):
            E.wait(t_co)
        V.wait(t_x)
        A.wait(t_x)

        def B(name):
            a, b = PR[name]
            o = PR["kvn"][0]
            return bc[:, a - o:b - o]

        def rstd(src, n, cols, junk, *w):
            ss = small(0, len(src))
            for i, s_ in enumerate(src):
                t = act(junk[i], s_, ACT.Square, w, acc=ss[:, i:i + 1])
            t = ts(cols, ss, 1.0 / n, 1e-6, ALU.mult, ALU.add, t)
            nh = C("nhalf")[:, 0:len(src)]
            return G.op(lambda e: e.tensor_tensor(cols, cols, nh, ALU.pow), t)

        def to_T(dst, src, nch, gname, *w):
            toks = []
            for c in range(0, nch, 2):
                b = PS.get()
                t = tr([(b[:, (2 * k + i) * 128:(2 * k + i) * 128 + 128],
                         src[:, i, (c + k) * 128:(c + k) * 128 + 128]) for k in range(2) for i in range(2)],
                       w, b.free)
                if gname is None:
                    E = V if c % 4 else A
                    u = [cp(E, dst[:, c:c + 2, :], b[:, :].rearrange("p (k t) -> p k t", k=2), t)]
                else:
                    u = []
                    for k in range(2):
                        o, g_ = dst[:, c + k, :], gain(gname, c + k)
                        if c % 4:
                            u.append(ts(o, b[:, 256 * k:256 * k + 256], g_, None, ALU.mult, None, t))
                        else:
                            u.append(act(o, b[:, 256 * k:256 * k + 256], ACT.Copy, t, scale=g_))
                PS.put(b, *u)
                toks += u
            return toks

        def norm(gname, src=X, *w):
            w = [w, T.last(), V.last(), A.last()]
            r = small(8, 2)
            t = rstd([src[:, 0, :], src[:, 1, :]], 1024, r, [Y[:, 0, :], Y[:, 1, :]], w)
            a = ts(Y[:, 0, :], src[:, 0, :], r[:, 0:1], None, ALU.mult, None, t)
            b = act(Y[:, 1, :], src[:, 1, :], ACT.Copy, t, scale=r[:, 1:2])
            return to_T(HT, Y, 8, gname, a, b)

        def wload(src, nk, n, *w):
            sl = WR.get()
            v = sl.buf[:, 0:nk * n].rearrange("p (k n) -> p k n", k=nk)
            t = sl.load(S, [(v, src.rearrange("(k p) n -> p k n", p=P))], *w)
            return sl, v, t

        def split(hi, src, lo, *w):
            k = src.shape[1] // 2
            out_ = []
            for s_ in (slice(0, k), slice(k, 2 * k)):
                t = cp(A, hi[:, s_], src[:, s_], *w)
                out_.append(tt(V, lo[:, s_], src[:, s_], hi[:, s_].bitcast(F32), ALU.subtract, t))
            return out_

        def pairs3(lf, lhs, rf, rhs, K):
            return [p for c in range(K) for p in ((lf(lhs[0], c), rf(rhs[0], c)), (lf(lhs[0], c), rf(rhs[1], c)),
                                                  (lf(lhs[1], c), rf(rhs[0], c)))]

        def sfeed(*specs):
            specs = list(specs)
            raw, cut = [], []

            def more():
                if specs:
                    raw.append(wload(*specs.pop(0)))

            def cut_one():
                if raw:
                    sl, v, t = raw.pop(0)
                    s2 = WR.get()
                    nk, n = v.shape[1], v.shape[2]
                    hi, lo = s2.rbuf[:, 0:nk * n], sl.rbuf[:, 0:nk * n]
                    toks = split(hi, sl.buf[:, 0:nk * n], lo, t, s2.free)
                    s2.free = [toks[-1]]
                    hv, lv = (a_.rearrange("p (k n) -> p k n", k=nk) for a_ in (hi, lo))
                    cut.append((Two(sl, s2), (hv, lv), toks))

            more()
            cut_one()
            more()

            def take():
                cut_one()
                more()
                return cut.pop(0)
            return take

        def evac_any(o, i, n, scale, *w):
            if n % 2:
                return ts(o, i, scale, None, ALU.mult, None, *w) if scale != 1.0 else cp(V, o, i, *w)
            return act(o, i, ACT.Copy, *w, scale=scale) if scale != 1.0 else cp(A, o, i, *w)

        cnt = [0]

        def proj_T(sl_v_t, lhs_of, nchunk, K, rhsT, dsts, w, fin=None):
            sl, v, tw = sl_v_t
            out_ = []
            for j in range(0, nchunk, 2):
                b = PS.get()
                m = min(2, nchunk - j)
                t = mm([(b[:, 256 * k:256 * k + 256],
                         pairs3(lambda v_, c, j=j, k=k: lhs_of(v_, c, j + k), v, lambda r, c: r[:, c, :], rhsT, K)
                         if isinstance(v, tuple) else [(lhs_of(v, c, j + k), rhsT[:, c, :]) for c in range(K)])
                        for k in range(m)], tw, w, b.free)
                cnt[0] += 1
                o, sc = dsts(j, m)
                if fin is not None:
                    u = fin(j, m, b, t)
                else:
                    u = evac_any(o, b[:, 0:256 * m].rearrange("p (k t) -> p k t", k=m), cnt[0], sc, t)
                PS.put(b, u)
                out_.append(u)
            return t, out_

        def proj_N(sl_v_t, c0, n, K, lT, dst, w):
            sl, v, tw = sl_v_t
            out_ = []
            for i in range(2):
                b = PS.get()
                t = mm([(b[:, 0:n],
                         pairs3(lambda l, c, i=i: l[:, c, 128 * i:128 * i + 128], lT,
                                lambda r, c: r[:, c, c0:c0 + n], v, K)
                         if isinstance(v, tuple) else
                         [(lT[:, c, 128 * i:128 * i + 128], v[:, c, c0:c0 + n]) for c in range(K)])],
                       tw, w, b.free)
                cnt[0] += 1
                u = evac_any(dst(i), b[:, 0:n], cnt[0], 1.0, t)
                PS.put(b, u)
                out_.append(u)
            return t, out_

        def cols(v, c, j):
            return v[:, c, 128 * j:128 * j + 128]

        def table(src, n, g):
            sl = CR.get()
            return sl, sl.buf[:, 0:n].rearrange("p (g n) -> p g n", g=g), sl.load(S, [(sl.buf[:, 0:n], src)])

        def attend(units, tbuf, pbuf, *w0):
            nt = len(tbuf)
            lag = nt - 1
            tfree = [[] for _ in range(nt)]
            pfree = [[], []]
            st = {}

            def scores(k):
                banks, bt = [], []
                for blk in units[k]["scores"]:
                    b = PS.get()
                    t = mm([(b[:, 256 * n:256 * n + 256], [qk]) for n, qk in enumerate(blk)], w0, b.free)
                    banks.append(b)
                    bt.append(t)
                return banks, bt

            def soften(k, banks, bt):
                u = units[k]
                tb = tbuf[k % nt]
                ends = []
                used = [[] for _ in banks]
                for g in u["soft"]:
                    mcol, first = g["m"], True
                    for (bi, c0, n, tab, tabtok, col0) in g["parts"]:
                        src = banks[bi][:, c0:c0 + n]
                        dst = tb[:, col0:col0 + n]
                        if tab is not None:
                            if len(tab.shape) == 3:
                                src = src.rearrange("p (k n) -> p k n", k=tab.shape[1])
                                dst = dst.rearrange("p (k n) -> p k n", k=tab.shape[1])
                            t = ttr(dst, src, tab, ALU.add, ALU.max, LOW if first else mcol, mcol,
                                    bt[bi], tabtok, tfree[k % nt])
                        else:
                            t = red(mcol, src, ALU.max, bt[bi], tfree[k % nt])
                        used[bi].append(t)
                        first = False
                    if g.get("done"):
                        g["done"](t)
                    if g.get("nsink") is not None:
                        t = ts(g["nm"], mcol, -1.0, g["nsink"], ALU.mult, ALU.min, t)
                    else:
                        t = ts(g["nm"], mcol, -1.0, None, ALU.mult, None, t)
                for g in u["soft"]:
                    a0, n = g["cols"]
                    if g["parts"][0][3] is None:
                        bi, c0 = g["parts"][0][0:2]
                        t = act(tb[:, a0:a0 + n], banks[bi][:, c0:c0 + n], ACT.Exp, t, tfree[k % nt],
                                bias=g["nm"], acc=g["den"])
                        used[bi].append(t)
                    else:
                        t = act(tb[:, a0:a0 + n], tb[:, a0:a0 + n], ACT.Exp, t, bias=g["nm"], acc=g["den"])
                    ends.append(t)
                for b, toks in zip(banks, used):
                    PS.put(b, *toks)
                st[k] = ends

            def turns(k):
                nb = units[k]["nblk"]
                tb = tbuf[k % nt]
                out_ = []
                for c in range(0, nb, 4):
                    m = min(4, nb - c)
                    b = PS.get()
                    t = tr([(b[:, 128 * n:128 * n + 128], tb[:, 128 * (c + n):128 * (c + n) + 128])
                            for n in range(m)], st[k], b.free)
                    out_.append((c, m, b, t))
                tfree[k % nt] = [t]
                return out_

            def turned(k, jobs):
                st[k] = []
                for c, m, b, t in jobs:
                    E = A if (k + c // 4) % 2 else V
                    u = cp(E, pbuf[:, k % 2, 128 * c:128 * (c + m)], b[:, 0:128 * m], t, pfree[k % 2])
                    PS.put(b, u)
                    st[k].append(u)

            def values(k):
                t = mm([(o, [(pbuf[:, k % 2, 128 * n:128 * n + 128], v) for n, v in prs])
                        for o, prs in units[k]["pv"]], st[k], units[k].get("ofree"))
                pfree[k % 2] = [t]
                if units[k].get("after"):
                    units[k]["after"](t)

            for k in range(len(units) + lag + 1):
                if k < len(units) and units[k].get("ahead"):
                    units[k]["ahead"]()
                sc = scores(k) if k < len(units) else None
                tn = turns(k - lag) if 0 <= k - lag < len(units) else None
                yield
                if sc is not None:
                    soften(k, *sc)
                if tn is not None:
                    turned(k - lag, tn)
                if k - lag >= 1:
                    values(k - lag - 1)

        def drain(gen):
            for _ in gen:
                pass

        def mixer(l):
            base = 0
            QK = ar[:, 0:22 * 256].rearrange("p (c t) -> p c t", c=22)
            VA = ar[:, 5632:7168].rearrange("p (i n) -> p i n", i=2)
            VW = ar[:, 7168:7680].rearrange("p (i n) -> p i n", i=2)
            GT = ar[:, 7680:11776].rearrange("p (c t) -> p c t", c=16)
            Hf = HT[:, :, :].rearrange("p c t -> p (c t)")
            tb = [ar[:, 11776:12544], ar[:, 14848:15616], ar[:, 15616:16384]]
            pb = ar[:, 13312:14848].rearrange("p (k n) -> p k n", k=2)
            OA = ar[:, 14848:15360].rearrange("p (i n) -> p i n", i=2)
            OAT = ar[:, 15360:15872].rearrange("p (c t) -> p c t", c=2)
            th = norm(f"norm_mix{l}")
            W = I["w_in"][l]
            th = [V.last(), A.last()]
            Hf = HT[:, :, :].rearrange("p c t -> p (c t)")
            th = split(YR[:, :, :].rearrange("p c t -> p (c t)"), Hf, HR[:, :, :].rearrange("p c t -> p (c t)"),
                       th, T.last())
            HH = (YR, HR)
            take = sfeed(*[(W[:, 512 * j:512 * j + 512], 8, 512) for j in range(4)], (W[:, 2048:2304], 8, 256),
                         *[(W[:, 2304 + 512 * j:2816 + 512 * j], 8, 512) for j in range(7)])
            ready = []
            for j in range(3):
                tile = take()
                t, o = proj_T(tile, cols, 4, 8, HH,
                              lambda a, m, j=j: (QK[:, 4 * j + a:4 * j + a + m, :], 0.125 if 4 * j + a < 6 else 1.0),
                              th)
                tile[0].free = [t]
                ready += o
            tile = take()
            t, o = proj_N(tile, 0, 512, 8, HH, lambda i: VA[:, i, 0:512], th)
            tile[0].free = [t]
            ready += o
            tile = take()
            t, o = proj_N(tile, 0, 256, 8, HH, lambda i: VA[:, i, 512:768], th)
            tile[0].free = [t]
            ready += o
            rd_dil = [V.last(), A.last()]

            for j in range(2):
                tile = take()
                t, o = proj_T(tile, cols, 4, 8, HH,
                              lambda a, m, j=j: (QK[:, 12 + 4 * j + a:12 + 4 * j + a + m, :], 0.125), th)
                tile[0].free = [t]
            tile = take()
            t, o = proj_T(tile, cols, 2, 8, HH, lambda a, m: (QK[:, 20:22, :], 1.0), th)
            t, o = proj_N(tile, 256, 256, 8, HH, lambda i: VW[:, i, :], th)
            tile[0].free = [t]
            rd_win = [V.last(), A.last()]

            def gates():
                held = None
                for j in range(4):
                    sl, v, tw = take()
                    for a in (0, 2, None) if j == 3 else (0, 2):
                        if a is not None:
                            b = PS.get()
                            t = mm([(b[:, 256 * k:256 * k + 256],
                                     pairs3(lambda v_, c, a=a, k=k: cols(v_, c, a + k), v, lambda r, c: r[:, c, :],
                                            HH, 8)) for k in range(2)], tw, th, b.free)
                        if held is not None:
                            c_, b_, t_ = held
                            for k in range(2):
                                u = act(GT[:, c_ + k, :], b_[:, 256 * k:256 * k + 256], ACT.Sigmoid, t_,
                                        bias=gain(f"bgate{l}", c_ + k))
                            PS.put(b_, u)
                        if a is not None:
                            held = (4 * j + a, b, t)
                            if a == 2:
                                sl.free = [t]
                            yield
            mx, nm, den = small(16, 8), small(24, 8), small(32, 8)
            units = []
            ob = [PS.get(), PS.get()]
            gots = [Late(lambda s=s: table(I["cd"][s], 1152, 3)) for s in range(4)]
            gots[0].get()
            for s in range(4):
                got = gots[s]
                for i in range(2):
                    qs = slice(128 * i, 128 * i + 128)
                    off = 128 * (1 - i)
                    hs = [4 * g + s for g in range(3)]
                    qk = [(QK[64 * (h % 2):64 * (h % 2) + 64, h // 2, qs],
                           QK[64 * (h % 2):64 * (h % 2) + 64, 6 + h // 2, :]) for h in hs]
                    n = 2 * s + i
                    u = {
                        "scores": [qk[0:2], qk[2:3]],
                        "soft": [{"m": mx[:, n:n + 1], "nm": nm[:, n:n + 1], "den": den[:, n:n + 1],
                                  "parts": Late(lambda got=got, off=off: [
                                      (0, 0, 512, got[1][:, 0:2, off:off + 256], got[2], 0),
                                      (1, 0, 256, got[1][:, 2, off:off + 256], got[2], 512)]),
                                  "cols": (0, 768)}],
                        "nblk": 6,
                        "pv": [(ob[i][:, 64 * s:64 * s + 64],
                                [(2 * g + k, VA[:, k, 64 * hs[g]:64 * hs[g] + 64]) for g in range(3) for k in range(2)])],
                        "ofree": ob[i].free,
                    }
                    if i == 0 and s < 3:
                        u["ahead"] = gots[s + 1].get
                    if i == 1:
                        u["soft"][0]["done"] = lambda t, got=got: setattr_free(got[0], t)
                    units.append(u)
            drain(attend(units, tb, pb, rd_dil, T.last()))
            tb = [ar[:, 11776:12288], ar[:, 14848:15360], ar[:, 15872:16384]]
            t = recip(den, den, A.last(), T.last())
            dv = den.rearrange("p (s i) -> p i s", i=2)
            for i in range(2):
                t = tt(V, OA[:, i, :].rearrange("p (s d) -> p s d", s=4),
                       ob[i][:, 0:256].rearrange("p (s d) -> p s d", s=4),
                       dv[:, i, :].unsqueeze(2).to_broadcast([P, 4, 64]), ALU.mult)
                PS.put(ob[i], t)
            toa = to_T(OAT, OA, 2, None, t)

            mx, nm, den, ns, es = small(48, 32), small(80, 32), small(112, 32), small(144, 16), small(160, 32)
            ts(ns, B(f"sink{l}"), -1.0, None, ALU.mult, None)
            ob2 = {}
            OB = ar[:, 0:2048].rearrange("p (i n) -> p i n", i=2)

            def flush(i, half, t):
                b = ob2.pop((i, half))
                lo = 16 * i + 8 * half
                a = tt(V, es[:, lo:lo + 8], B(f"sink{l}")[:, 8 * half:8 * half + 8], nm[:, lo:lo + 8], ALU.add, A.last())
                a = act(es[:, lo:lo + 8], es[:, lo:lo + 8], ACT.Exp, a)
                a = tt(V, den[:, lo:lo + 8], den[:, lo:lo + 8], es[:, lo:lo + 8], ALU.add, a)
                a = recip(den[:, lo:lo + 8], den[:, lo:lo + 8])
                a = tt(V, OB[:, i, 512 * half:512 * half + 512].rearrange("p (s d) -> p s d", s=8),
                       b[:, :].rearrange("p (s d) -> p s d", s=8),
                       den[:, lo:lo + 8].unsqueeze(2).to_broadcast([P, 8, 64]), ALU.mult, t)
                PS.put(b, a)

            def win_unit(i, hp, got, bank):
                qs = slice(128 * i, 128 * i + 128)
                off = 128 * (1 - i)
                hs = [2 * hp, 2 * hp + 1]
                kv = hs[0] // 4
                bp = 64 * (kv % 2)
                qk = []
                for h in hs:
                    c = 12 + 4 * (h // 8) + h % 4
                    qk.append((QK[bp:bp + 64, c, qs], QK[bp:bp + 64, 20 + kv // 2, :]))
                soft = []
                for n, h in enumerate(hs):
                    x = 16 * i + h
                    soft.append({"m": mx[:, x:x + 1], "nm": nm[:, x:x + 1], "den": den[:, x:x + 1],
                                 "parts": Late(lambda n=n, h=h: [(0, 256 * n, 256, got[1][:, h % 4, off:off + 256], got[2],
                                                                  256 * n)]),
                                 "cols": (256 * n, 256), "nsink": ns[:, h:h + 1]})
                if hp % 2:
                    soft[1]["done"] = lambda t: setattr_free(got[0], t)
                return {
                    "scores": [qk], "soft": soft, "nblk": 4,
                    "pv": [(bank[:, 64 * (h % 8):64 * (h % 8) + 64],
                            [(2 * n + k, VW[:, k, 64 * kv:64 * kv + 64]) for k in range(2)])
                           for n, h in enumerate(hs)],
                    "ofree": bank.free,
                }

            us = []
            gots = [Late(lambda n=n: table(I["cw"][n % 4], 1536, 4)) for n in range(8)]
            gots[0].get()
            for i in range(2):
                for half in range(2):
                    bank = PS.get()
                    ob2[(i, half)] = bank
                    for gq in range(2 * half, 2 * half + 2):
                        n = 4 * i + gq
                        for hp in (2 * gq, 2 * gq + 1):
                            us.append(win_unit(i, hp, gots[n], bank))
                        if n < 7:
                            us[-2]["ahead"] = gots[n + 1].get
                    us[-1]["after"] = lambda t, i=i, half=half: flush(i, half, t)
            side = gates()
            for _ in attend(us, tb, pb, rd_win, T.last(), V.last()):
                next(side, None)
            drain(side)
            OBT = HT
            tob = to_T(OBT, OB, 8, None, V.last(), T.last())
            MT = Y[:, :, :].rearrange("p i (c t) -> p (i c) t", t=256)
            wa = wload(I["w_branch_a"][l], 2, 1024)
            wbs = []
            ready = [V.last(), A.last(), T.last()]
            ya_tok = []
            for j in range(0, 8, 2):
                b = PS.get()
                t = mm([(b[:, 256 * k:256 * k + 256], [(wa[1][:, c, 128 * (j + k):128 * (j + k) + 128], OAT[:, c, :])
                                                       for c in range(2)]) for k in range(2)], wa[2], ready, b.free)
                u = tt(V, MT[:, j:j + 2, :], b[:, :].rearrange("p (k t) -> p k t", k=2), GT[:, j:j + 2, :], ALU.mult, t)
                PS.put(b, u)
            wa[0].free = [t]
            for half in range(2):
                wb = wload(I["w_branch_b"][l][:, 512 * half:512 * half + 512], 8, 512)
                for j in range(0, 4, 2):
                    b = PS.get()
                    t = mm([(b[:, 256 * k:256 * k + 256], [(cols(wb[1], c, j + k), OBT[:, c, :])
                                                           for c in range(8)]) for k in range(2)], wb[2], b.free)
                    jj = 4 * half + j
                    tmp = ar[:, 11776 + 512 * ((j // 2) % 2):12288 + 512 * ((j // 2) % 2)].rearrange("p (k t) -> p k t", k=2)
                    u = tt(V, tmp, b[:, :].rearrange("p (k t) -> p k t", k=2), GT[:, 8 + jj:10 + jj, :], ALU.mult, t)
                    PS.put(b, u)
                    u = tt(V, MT[:, jj:jj + 2, :], MT[:, jj:jj + 2, :], tmp, ALU.add)
                wb[0].free = [t]
            residual(MT, I["w_out"][l], u)

        def setattr_free(sl, t):
            sl.free = [t]

        def residual(MT, W, *w):
            for half in range(2):
                wo = wload(W[:, 512 * half:512 * half + 512], 8, 512)
                for i in range(2):
                    b = PS.get()
                    t = mm([(b[:, :], [(MT[:, c, 128 * i:128 * i + 128], wo[1][:, c, :]) for c in range(8)])],
                           wo[2], b.free, *w)
                    x = X[:, i, 512 * half:512 * half + 512]
                    PS.put(b, tt(V, x, x, b[:, :], ALU.add, t))
                wo[0].free = [t]

        zt = []

        def experts(l, extra):
            PA = ar[:, 0:1024].rearrange("p (i n) -> p i n", i=2)
            PG = ar[:, 1024:2048].rearrange("p (i n) -> p i n", i=2)
            PT = ar[:, 2048:3072].rearrange("p (g t) -> p g t", g=4)
            XE = ar[:, 3072:7168].rearrange("p (c n) -> p c n", c=8)
            wr = ar[:, 7168:7296].rearrange("p (c n) -> p c n", c=8)
            SI = ar[:, 7296:9344].rearrange("p (k n) -> p k n", k=2)
            AT = ar[:, 9344:11392].rearrange("p (k c n) -> p k c n", k=2, c=8)
            YE = ar[:, 11392:12416]
            af = ar[:, 12416:12448].rearrange("p (i n) -> p i n", i=2)
            mk = ar[:, 12448:12480].rearrange("p (i n) -> p i n", i=2)
            ky = ar[:, 12480:12512].rearrange("p (i n) -> p i n", i=2)
            aT = ar[0:16, 12544:12800]
            wk = [ar[0:16, 12800:13056], ar[0:16, 13056:13312]]
            mT = ar[0:16, 13312:13568]
            t8 = ar[0:16, 13568:13576]
            twr = one[2].load(S, [(wr, I["w_router"][l].rearrange("(c p) n -> p c n", p=P))], T.last(), V.last(), A.last())
            th = norm(f"norm_ffn{l}")
            m1, s1 = small(16, 2), small(18, 2)
            b = PS.get()
            for i in range(2):
                t = mm([(b[:, 16 * i:16 * i + 16], [(HT[:, c, 128 * i:128 * i + 128], wr[:, c, :]) for c in range(8)])],
                       th, twr, b.free)
            red(m1, b[:, 0:32].rearrange("p (i n) -> p i n", i=2), ALU.max, t)
            u = ts(m1, m1, -1.0, None, ALU.mult, None)
            for i in range(2):
                u = act(af[:, i, :], b[:, 16 * i:16 * i + 16], ACT.Exp, u, bias=m1[:, i:i + 1], acc=s1[:, i:i + 1])
            recip(s1, s1, u)
            for i in range(2):
                u = ts(af[:, i, :], af[:, i, :], s1[:, i:i + 1], None, ALU.mult, None)
            t = tr([(b[0:16, 128 + 128 * i:256 + 128 * i], af[:, i, :]) for i in range(2)], u)
            cp(V, aT, b[0:16, 128:384], t)
            src = aT
            for r in range(4):
                dst = wk[r % 2]
                V.op(lambda e, s=src: e.max(t8, s))
                u = V.op(lambda e, s=src, d=dst: e.match_replace(d, t8, s, -1.0))
                src = dst
            u = ts(mT, src, 0.0, None, ALU.is_lt, None)
            PS.put(b, u)
            b = PS.get()
            t = tr([(b[:, 16 * i:16 * i + 16], mT[:, 128 * i:128 * i + 128]) for i in range(2)], u, b.free)
            u = cp(V, mk, b[:, 0:32].rearrange("p (i n) -> p i n", i=2), t)
            t = mm([(b[:, 64:80], [(C("ustr"), mk[:, 0, :])]),
                    (b[:, 80:96], [(C("ones"), mk[:, 0, :]), (C("ustr"), mk[:, 1, :])])], u)
            u = stt(ky, b[:, 64:96].rearrange("p (i n) -> p i n", i=2), 1.0, mk, ALU.add, ALU.mult, t)
            PS.put(b, u)
            ts(ky, ky, 1.0, None, ALU.subtract, None)
            for i in range(2):
                pv = PA[:, i, :].rearrange("p (e c) -> p e c", e=16)
                u = tt(V, pv, C("iota").unsqueeze(1).to_broadcast([P, 16, 32]),
                       ky[:, i, :].unsqueeze(2).to_broadcast([P, 16, 32]), ALU.is_equal)
            tpa = u
            for i in range(2):
                u = tt(V, PG[:, i, :].rearrange("p (e c) -> p e c", e=16), PA[:, i, :].rearrange("p (e c) -> p e c", e=16),
                       af[:, i, :].unsqueeze(2).to_broadcast([P, 16, 32]), ALU.mult)
            tpg = u
            xe_t = []
            for c in range(8):
                b = PS.get()
                t = mm([(b[:, :], [(Y[:, i, 128 * c:128 * c + 128], PA[:, i, :]) for i in range(2)])], tpa, b.free)
                if c % 2:
                    u = ts(XE[:, c, :], b[:, :], gain(f"norm_ffn{l}", c), None, ALU.mult, None, t)
                else:
                    u = act(XE[:, c, :], b[:, :], ACT.Copy, t, scale=gain(f"norm_ffn{l}", c))
                PS.put(b, u)
                xe_t.append(u)
            for g in range(0, 4, 2):
                b = PS.get()
                t = tr([(b[:, 256 * k + 128 * i:256 * k + 128 * i + 128], PG[:, i, 128 * (g + k):128 * (g + k) + 128])
                        for k in range(2) for i in range(2)], tpg, b.free)
                u = cp(V if g else A, PT[:, g:g + 2, :], b[:, :].rearrange("p (k t) -> p k t", k=2), t)
                PS.put(b, u)
                xe_t.append(u)
            xe_t = xe_t[-4:]


            def gate_up(g):
                banks = {}
                for name, Wn in (("a", "w_expert_gate"), ("u", "w_expert_up")):
                    bs = [PS.get(), PS.get()]
                    for k in range(4):
                        e_ = 4 * g + k
                        tl = [wload(I[Wn][l, e_, 512 * h:512 * h + 512, :], 4, 1024) for h in range(2)]
                        for h in range(2):
                            def f(e, h=h, k=k, e_=e_, tl=tl, bs=bs):
                                for n in range(2):
                                    for c in range(4):
                                        m = e.matmul(bs[n][32 * k:32 * k + 32, :],
                                                     XE[:, 4 * h + c, 32 * e_:32 * e_ + 32],
                                                     tl[h][1][:, c, 512 * n:512 * n + 512],
                                                     start=(h == 0 and c == 0), stop=(h == 1 and c == 3),
                                                     tile_position=(0, 32 * k))
                                return m
                            t = T.op(f, tl[h][2], xe_t, bs[0].free, bs[1].free)
                            tl[h][0].free = [t]
                    banks[name] = (bs, t)
                ab, ta = banks["a"]
                ub, tu = banks["u"]
                s_ = SI[:, g % 2, :]
                for n in range(2):
                    u = act(s_[:, 512 * n:512 * n + 512], ab[n][:, :], ACT.Silu, ta)
                    PS.put(ab[n], u)
                for n in range(2):
                    v = tt(V, s_[:, 512 * n:512 * n + 512], s_[:, 512 * n:512 * n + 512], ub[n][:, :], ALU.mult, u, tu)
                    PS.put(ub[n], v)
                return v

            def turn(g, v):
                us = []
                for c in range(0, 8, 4):
                    b = PS.get()
                    t = tr([(b[:, 128 * k:128 * k + 128], SI[:, g % 2, 128 * (c + k):128 * (c + k) + 128])
                            for k in range(4)], v, b.free)
                    u = cp(V if c else A, AT[:, g % 2, c:c + 4, :], b[:, :].rearrange("p (k n) -> p k n", k=4), t)
                    PS.put(b, u)
                    us.append(u)
                return us

            def down(g, us):
                bs = [PS.get(), PS.get()]
                for k in range(4):
                    e_ = 4 * g + k
                    tl = [wload(I["w_expert_down"][l, e_, 512 * h:512 * h + 512, :], 4, 1024) for h in range(2)]
                    for h in range(2):
                        def f(e, h=h, k=k, tl=tl):
                            for n in range(2):
                                for c in range(4):
                                    m = e.matmul(bs[n][32 * k:32 * k + 32, :], AT[:, g % 2, 4 * h + c, 32 * k:32 * k + 32],
                                                 tl[h][1][:, c, 512 * n:512 * n + 512],
                                                 start=(h == 0 and c == 0), stop=(h == 1 and c == 3),
                                                 tile_position=(0, 32 * k))
                            return m
                        t = T.op(f, tl[h][2], us, bs[0].free, bs[1].free)
                        tl[h][0].free = [t]
                us = []
                for n in range(2):
                    u = cp(A if n else V, YE[:, 512 * n:512 * n + 512], bs[n][:, :], t)
                    PS.put(bs[n], u)
                    us.append(u)
                for i in range(2):
                    for n in range(2):
                        b = PS.get()
                        t = mm([(b[:, :], [(PT[:, g, 128 * i:128 * i + 128], YE[:, 512 * n:512 * n + 512])])], us, b.free)
                        x = X[:, i, 512 * n:512 * n + 512]
                        PS.put(b, tt(V, x, x, b[:, :], ALU.add, t))

            prev = None
            for g in range(4):
                v = gate_up(g)
                next(extra, None)
                if prev is not None:
                    down(g - 1, prev)
                prev = turn(g, v)
            down(3, prev)
            for _ in extra:
                pass

        KM = [cbuf[:, l, 0:512].rearrange("p (c t) -> p c t", c=2) for l in range(2)]
        VM = [cbuf[:, l, 512:1024].rearrange("p (i n) -> p i n", i=2) for l in range(2)]

        def rel_tables():
            oh = ar[0:32, 13824:14335]
            rb = small(480, 12)[0:32, :]
            t0 = one[3].load(S, [(oh, I["oh"]), (rb, I["rel_bias_2"])], V.last(), A.last(), T.last(), G.last())
            w = None
            for q in range(3):
                us = []
                for h in range(4):
                    b = PS.get()
                    t = mm([(b[:, 0:511], [(rb[:, 4 * q + h:4 * q + h + 1].to_broadcast([32, 128]), oh)])], t0, b.free)
                    u = cp(A if h % 2 else V, ar[:, 14336 + 512 * h:14336 + 512 * h + 511], b[:, 0:511], t, w)
                    PS.put(b, u)
                    us.append(u)
                w = one[4].load(A, [(zd[4 * q + h, :, 0:511], ar[:, 14336 + 512 * h:14336 + 512 * h + 511])
                                    for h in range(4)], us)
                yield
            zt.append(w)
            for E in (V, A):
                E.wait(w)

        def memory():
            last = [T.last(), V.last(), A.last(), G.last()]
            t = one[5].load(S, [(Y[:, :, :], I["mem_2"][0].rearrange("(i p) n -> p i n", p=P))], last)
            r = small(232, 2)
            junk = ar[:, 15360:16384]
            u = rstd([Y[:, 0, :], Y[:, 1, :]], 1024, r, [junk, junk], t)
            a = ts(Y[:, 0, :], Y[:, 0, :], r[:, 0:1], None, ALU.mult, None, u)
            b = act(Y[:, 1, :], Y[:, 1, :], ACT.Copy, u, scale=r[:, 1:2])
            th = to_T(HT, Y, 8, "mem", a, b, last)
            yield
            for l in range(2):
                tile = wload(I["w_mem_kv_2"][l], 8, 512)
                proj_T(tile, cols, 2, 8, HT, lambda a, m, l=l: (KM[l], 1.0), th)
                t, o = proj_N(tile, 256, 256, 8, HT, lambda i, l=l: VM[l][:, i, :], th)
                tile[0].free = [t]
                yield

        def bcast_row(name, dst, s, *w):
            a, b = PR[name]
            return s.load(S, [(dst, I["pr"][0:1, a:b].to_broadcast([P, b - a]))], *w)

        def row_norm(name, dst, slot):
            gb = ar[:, 15360:16384]
            tg = bcast_row(name, gb, slot, V.last(), A.last(), T.last(), G.last())
            r = small(8, 2)
            t = rstd([X[:, 0, :], X[:, 1, :]], 1024, r, [Y[:, 0, :], Y[:, 1, :]], V.last(), T.last())
            for i in range(2):
                t = stt(dst[:, i, :], X[:, i, :], r[:, i:i + 1], gb, ALU.mult, ALU.mult, t, tg, A.last())
            return t

        def mem_units(l, QM, OM, ob, tiles):
            mx, nm, den = small(208, 8), small(216, 8), small(224, 8)
            us = []
            for i in range(tiles):
                for hp in range(2):
                    qs = slice(128 * i, 128 * i + 128)
                    qk, soft = [], []
                    for n in range(2):
                        h = 2 * hp + n
                        x = 4 * i + h
                        qk.append((QM[64 * n:64 * n + 64, hp, qs], KM[l][64 * n:64 * n + 64, hp, :]))
                        soft.append({"m": mx[:, x:x + 1], "nm": nm[:, x:x + 1], "den": den[:, x:x + 1],
                                     "parts": [(n, 0, 256, None, None, 256 * n)], "cols": (256 * n, 256)})
                    us.append({"scores": [qk[0:1], qk[1:2]], "soft": soft, "nblk": 4,
                               "pv": [(ob[:, 256 * i + 64 * (2 * hp + n):256 * i + 64 * (2 * hp + n) + 64],
                                       [(2 * n + k, VM[l][:, k, 64 * (2 * hp + n):64 * (2 * hp + n) + 64]) for k in range(2)])
                                      for n in range(2)], "ofree": ob.free})

            def flush():
                n = 4 * tiles
                recip(den[:, 0:n], den[:, 0:n], A.last(), T.last())
                for i in range(tiles):
                    t = tt(V, OM[:, i, :].rearrange("p (s d) -> p s d", s=4),
                           ob[:, 256 * i:256 * i + 256].rearrange("p (s d) -> p s d", s=4),
                           den[:, 4 * i:4 * i + 4].unsqueeze(2).to_broadcast([P, 4, 64]), ALU.mult)
                PS.put(ob, t)
                return t
            return us, flush

        def mix_a(zt, tmem):
            l = 0
            QT = ar[:, 0:1536].rearrange("p (c t) -> p c t", c=6)
            KT = ar[:, 1536:3072].rearrange("p (c t) -> p c t", c=6)
            VV = ar[:, 3072:4608].rearrange("p (i n) -> p i n", i=2)
            IQ = ar[:, 4608:5632].rearrange("p (c t) -> p c t", c=4)
            IK = ar[:, 5632:5888]
            QM = ar[:, 5888:6400].rearrange("p (c t) -> p c t", c=2)
            CK = ar[:, 6400:6912].rearrange("p (i n) -> p i n", i=2)
            CT = ar[:, 6912:7424].rearrange("p (c t) -> p c t", c=2)
            BH = ar[:, 7424:12032].rearrange("p (h n) -> p h n", h=12)
            Hf = HT[:, :, :].rearrange("p c t -> p (c t)")
            tb = [Hf[:, 512 * k:512 * k + 512] for k in range(3)]
            pb = ar[:, 13056:14080].rearrange("p (k n) -> p k n", k=2)
            SC = ar[:, 14080:14592].rearrange("p (i n) -> p i n", i=2)
            RL = ar[:, 14592:15104].rearrange("p (i n) -> p i n", i=2)
            BM = ar[:, 15104:16128].rearrange("p (k n) -> p k n", k=4)
            IW = small(240, 16).rearrange("p (i n) -> p i n", i=2)
            t8 = small(256, 8)
            th = norm("mix20")
            tbh = one[6].load(S, [(BH[:, h, :], bass.AP(tensor=zd.tensor, offset=h * 65536 + 127,
                                                         ap=[[511, 128], [1, 384]])) for h in range(12)],
                              zt, T.last(), V.last(), A.last())
            W = I["a_w_in_2"][0]
            tile = wload(W[:, 0:512], 8, 512)
            t, o = proj_T(tile, cols, 4, 8, HT, lambda a, m: (QT[:, a:a + m, :], 0.125), th)
            tile[0].free = [t]
            tile = wload(W[:, 512:1024], 8, 512)
            t, o = proj_T(tile, cols, 2, 8, HT, lambda a, m: (QT[:, 4:6, :], 0.125), th)
            t, o = proj_N(tile, 256, 256, 8, HT, lambda i: CK[:, i, :], th)
            tile[0].free = [t]
            tile = wload(W[:, 1024:1536], 8, 512)
            t, o = proj_T(tile, cols, 4, 8, HT, lambda a, m: (IQ[:, a:a + m, :], 0.125), th)
            tile[0].free = [t]
            tile = wload(W[:, 1536:1864], 8, 328)
            sl, v, tw = tile
            b = PS.get()
            t = mm([(b[0:64, 0:256], [(v[:, c, 0:64], HT[:, c, :]) for c in range(8)])], tw, th, b.free)
            t = mm([(b[64:128, 0:256], [(v[:, c, 0:64], HT[:, c, :]) for c in range(8)])])
            u = cp(A, IK, b[:, 0:256], t)
            PS.put(b, u)
            b = PS.get()
            t = mm([(b[:, 8 * i:8 * i + 8], [(HT[:, c, 128 * i:128 * i + 128], v[:, c, 64:72]) for c in range(8)])
                    for i in range(2)], b.free)
            u = ts(IW, b[:, 0:16].rearrange("p (i n) -> p i n", i=2), 8.0 ** -0.5, None, ALU.mult, None, t)
            PS.put(b, u)
            t, o = proj_T(tile, lambda v, c, j: v[:, c, 72 + 128 * j:200 + 128 * j], 2, 8, HT,
                          lambda a, m: (QM, 0.125), th)
            sl.free = [t]
            r = small(8, 2)
            t = rstd([CK[:, 0, :], CK[:, 1, :]], 256, r, [SC[:, 0, :], SC[:, 1, :]], V.last())
            for i in range(2):
                t = stt(CK[:, i, :], CK[:, i, :], r[:, i:i + 1], B("kvn"), ALU.mult, ALU.mult, t, A.last())
            tct = to_T(CT, CK, 2, None, t)
            tct = [V.last(), A.last()]
            wk_ = wload(I["uk"], 2, 768)
            for j in range(0, 6, 2):
                b = PS.get()
                t = mm([(b[:, 256 * k:256 * k + 256], [(wk_[1][:, c, 128 * (j + k):128 * (j + k) + 128], CT[:, c, :])
                                                       for c in range(2)]) for k in range(2)], wk_[2], tct, b.free)
                u = cp(A, KT[:, j:j + 2, :], b[:, :].rearrange("p (k t) -> p k t", k=2), t)
                PS.put(b, u)
            wk_[0].free = [t]
            wv_ = wload(I["uv"], 2, 768)
            for i in range(2):
                for c0, n in ((0, 512), (512, 256)):
                    b = PS.get()
                    t = mm([(b[:, 0:n], [(CT[:, c, 128 * i:128 * i + 128], wv_[1][:, c, c0:c0 + n]) for c in range(2)])],
                           wv_[2], b.free)
                    u = cp(A, VV[:, i, c0:c0 + n], b[:, 0:n], t)
                    PS.put(b, u)
            wv_[0].free = [t]
            rl_free = [[], []]
            for i in range(2):
                for hp in range(4):
                    bs = [PS.get(), PS.get()]
                    t = mm([(bs[n][:, 0:256], [(IQ[64 * n:64 * n + 64, hp, 128 * i:128 * i + 128],
                                                IK[64 * n:64 * n + 64, :])]) for n in range(2)],
                           V.last() if hp == 0 else None, A.last() if hp == 0 else None, bs[0].free, bs[1].free)
                    for n in range(2):
                        h = 2 * hp + n
                        u = act(RL[:, n, :], bs[n][:, 0:256], ACT.Relu, t, rl_free[n])
                        PS.put(bs[n], u)
                        in1 = SC[:, i, :] if h else C("causal")[:, 256 * i:256 * i + 256]
                        x = stt(SC[:, i, :], RL[:, n, :], IW[:, i, h:h + 1], in1, ALU.mult, ALU.add, u)
                        rl_free[n] = [x]
            OM = Y[:, :, 768:1024]
            ob = PS.get()
            mu, mflush = mem_units(l, QM, OM, ob, 2)
            side = attend(mu, tb, pb, V.last(), A.last(), T.last(), tmem)
            mask = []
            for i in range(2):
                src = SC[:, i, :]
                for r_ in range(8):
                    if r_ % 2 == 0:
                        next(side, None)
                    dst = RL[:, r_ % 2, :]
                    V.op(lambda e, s=src: e.max(t8, s))
                    V.op(lambda e, s=src, d=dst: e.match_replace(d, t8, s, LOW))
                    src = dst
                ts(SC[:, i, :], src, -2.0e38, NEG, ALU.is_ge, ALU.mult)
                mask.append(tt(V, SC[:, i, :], SC[:, i, :], C("causal")[:, 256 * i:256 * i + 256], ALU.add))
            mx, nm, den = small(16, 24), small(40, 24), small(64, 24)
            OS = Y[:, :, 0:768]
            bmfree = [[] for _ in range(4)]
            nb = [0]
            ops = {}
            drain(side)
            mflush()
            us = []
            for i in range(2):
                obs = [PS.get(), PS.get()]
                for hp in range(6):
                    qs = slice(128 * i, 128 * i + 128)
                    off = 128 * (1 - i)
                    qk, soft = [], []
                    for n in range(2):
                        h = 2 * hp + n
                        x = 12 * i + h
                        s_ = nb[0] % 4
                        nb[0] += 1
                        tbm = [None]
                        qk.append((QT[64 * n:64 * n + 64, hp, qs], KT[64 * n:64 * n + 64, hp, :]))
                        soft.append({"m": mx[:, x:x + 1], "nm": nm[:, x:x + 1], "den": den[:, x:x + 1],
                                     "mk": (s_, h, i, off), "cols": (256 * n, 256)})
                    us.append({"scores": [qk[0:1], qk[1:2]], "soft": soft, "nblk": 4,
                               "pv": [(obs[h // 8][:, 64 * (h % 8):64 * (h % 8) + 64],
                                       [(2 * n + k, VV[:, k, 64 * h:64 * h + 64]) for k in range(2)])
                                      for n, h in ((0, 2 * hp), (1, 2 * hp + 1))],
                               "ofree": [obs[0].free, obs[1].free]})
                for u_ in us[-6:]:
                    for n, g in enumerate(u_["soft"]):
                        s_, h, i_, off_ = g["mk"]
                        g["parts"] = Late(lambda s_=s_, h=h, i_=i_, off_=off_, n=n: [(
                            n, 0, 256, BM[:, s_, :],
                            tt(G, BM[:, s_, :], BH[:, h, off_:off_ + 256], SC[:, i_, :], ALU.add, tbh, mask[i_], bmfree[s_]),
                            256 * n)])
                        g["done"] = lambda t, s_=s_: bmfree.__setitem__(s_, [t])

                def flush(t, i=i, obs=obs):
                    dn = den[:, 12 * i:12 * i + 12]
                    recip(dn, dn, A.last())
                    for b_, (h0, nh) in zip(obs, ((0, 8), (8, 4))):
                        PS.put(b_, tt(V, OS[:, i, 64 * h0:64 * (h0 + nh)].rearrange("p (s d) -> p s d", s=nh),
                                      b_[:, 0:64 * nh].rearrange("p (s d) -> p s d", s=nh),
                                      dn[:, h0:h0 + nh].unsqueeze(2).to_broadcast([P, nh, 64]), ALU.mult, t))
                us[-1]["after"] = flush
            drain(attend(us, tb, pb, V.last(), A.last(), T.last()))
            to_T(HT, Y, 8, None, V.last(), T.last())
            residual(HT, I["w_o_2"][0], V.last(), A.last())

        QT = ar[:, 0:4096].rearrange("p (c t) -> p c t", c=16)
        KS = [ar[:, a:a + 256].rearrange("p (i n) -> p i n", i=2) for a in (4096, 7936)]
        GA = ar[:, 6656:6912].rearrange("p (i n) -> p i n", i=2)
        IX = arU[:, 6912:7168].rearrange("p (i n) -> p i n", i=2)
        DT = ar[:, 7168:7424].rearrange("p (i n) -> p i n", i=2)
        DG = ar[:, 7424:7936].rearrange("p (k n) -> p k n", k=4)
        JK = ar[:, 14336:15360]
        gb = ar[:, 15360:16384]

        def feed(*specs):
            specs = list(specs)
            cur = [wload(*specs.pop(0))]

            def take():
                t = cur.pop()
                if specs:
                    cur.append(wload(*specs.pop(0)))
                return t
            return take

        def rstd_row(src, n, junk, *w):
            m, y, z = small(424, 1), small(425, 1), small(426, 1)
            t = act(junk, src, ACT.Square, V.last(), w, acc=m)
            t = ts(m, m, 1.0 / n, 1e-6, ALU.mult, ALU.add, t)
            t = act(y, m, ACT.Sqrt, t)
            recip(y, y, t)
            tt(V, z, y, y, ALU.mult)
            tt(V, z, z, m, ALU.mult)
            ts(z, z, -0.5, 1.5, ALU.mult, ALU.add)
            return y, tt(V, y, y, z, ALU.mult)

        def turn_tile(i, parts, *w):
            jobs = []
            for src, c0, n, gname in parts:
                for c in range(0, n, 4):
                    m = min(4, n - c)
                    b = PS.get()
                    t = tr([(b[:, 128 * k:128 * k + 128], src[:, 128 * (c + k):128 * (c + k) + 128]) for k in range(m)],
                           w, b.free)
                    jobs.append((b, t, c0 + c, m, None if gname is None else PF[gname][0] + c))
            yield
            for b, t, c, m, g0 in jobs:
                o = HT[:, c:c + m, 128 * i:128 * i + 128]
                bv = b[:, 0:128 * m].rearrange("p (k t) -> p k t", k=m)
                if g0 is None:
                    u = cp(A, o, bv, t)
                else:
                    u = tt(V, o, bv, pf[:, g0:g0 + m].unsqueeze(2).to_broadcast([P, m, 128]), ALU.mult, t)
                PS.put(b, u)

        def norm_tile(i, gname):
            r, t = rstd_row(X[:, i, :], 1024, Y[:, i, :], T.last())
            t = act(Y[:, i, :], X[:, i, :], ACT.Copy, t, scale=r)
            yield from turn_tile(i, [(Y[:, i, :], 0, 8, gname)], t)

        def chunks_tile(i, v, c0, n, w):
            b = PS.get()
            t = mm([(b[:, 128 * k:128 * k + 128],
                     [(v[:, c, c0 + 128 * k:c0 + 128 * k + 128], HT[:, c, 128 * i:128 * i + 128]) for c in range(8)])
                    for k in range(n)], w, b.free)
            return b, t

        def residual_tile(i, take):
            old = None
            for half in range(3):
                if half < 2:
                    sl, v, tw = take()
                    b = PS.get()
                    t = mm([(b[:, :], [(HT[:, c, 128 * i:128 * i + 128], v[:, c, :]) for c in range(8)])],
                           tw, b.free, V.last(), A.last())
                    sl.free = [t]
                if old is not None:
                    h_, b_, t_ = old
                    x = X[:, i, 512 * h_:512 * h_ + 512]
                    PS.put(b_, tt(V, x, x, b_[:, :], ALU.add, t_))
                old = (half, b, t)
                if half < 2:
                    yield
                    yield

        def mix_b(i):
            XD = ar[:, 8192:9728].rearrange("p (i n) -> p i n", i=2)
            ZT = ar[:, 9728:10496]
            XR = ar[:, 10496:11806].rearrange("p (c t) -> p c t", c=10)
            CB = ar[:, 10496:11008].rearrange("p (g n) -> p g n", g=2)
            TR = ar[:, 11008:11776]
            XC = ar[:, 11806:13086].rearrange("p (c t) -> p c t", c=10)
            XS = ar[:, 13086:13854]
            tb = [ar[:, 11806:12318], ar[:, 12318:12830]]
            pb = ar[:, 12830:13854].rearrange("p (k n) -> p k n", k=2)
            B0 = ar[:, 13854:14110].rearrange("p (g n) -> p g n", g=2)
            TL = ar[:, 14110:14140].rearrange("p (c n) -> p c n", c=10)
            EE = cbuf[:, 0, 0:1024].rearrange("p (k h n) -> p k h n", k=2, h=2)
            TM = cbuf[:, 0, 1024:1536].rearrange("p (k h n) -> p k h n", k=2, h=2)
            QM = cbuf[:, 0, 0:256].rearrange("p (c t) -> p c t", c=2)
            dt, da, nac, u1, u2, ng = (small(256 + 12 * k, 12) for k in range(6))
            eb = small(412, 12)
            OM = Y[:, :, 768:1024]
            Hi = [HT[:, c, 128 * i:128 * i + 128] for c in range(8)]
            W = I["b_w_in_2"][0]
            take = feed((W[:, 2048:2316], 8, 268))
            yield from norm_tile(i, "mix21")
            th = [V.last(), A.last()]
            sl, v, tw = take()
            b, t = chunks_tile(i, v, 12, 2, [tw, th])
            b2 = PS.get()
            t2 = mm([(b2[:, 0:12], [(Hi[c], v[:, c, 0:12]) for c in range(8)])], b2.free)
            sl.free = [t2]
            yield
            u = ts(QM, b[:, 0:256].rearrange("p (c t) -> p c t", c=2), 0.125, None, ALU.mult, None, t, A.last())
            PS.put(b, u)
            t = tt(V, u1, b2[:, 0:12], B("dtb"), ALU.add, t2)
            PS.put(b2, t)
            ts(u2, u1, -1.0, None, ALU.mult, None)
            t = tt(V, u2, u2, u1, ALU.min)
            act(u2, u2, ACT.Exp, t)
            act(u2, u2, ACT.Ln, bias=1.0)
            t2 = act(ng, B("alog"), ACT.Exp)
            yield
            stt(dt, u1, 0.0, u2, ALU.max, ALU.add, t2)
            stt(da, dt, -1.0, ng, ALU.mult, ALU.mult)
            b = PS.get()
            t = mm([(b[:, 0:12], [(C("uinc"), da)])] + ([(b[:, 12:24], [(C("ones"), da)])] if i == 0 else []),
                   V.last(), b.free)
            ob = PS.get()
            mu, mflush = mem_units(1, QM, OM[:, i:i + 1, :], ob, 1)
            at = attend(mu, tb, pb, V.last(), A.last(), T.last())
            next(at)
            yield
            u = ts(nac, b[:, 0:12], -1.0, None, ALU.mult, None, t)
            if i == 0:
                u = tt(V, eb, b[:, 12:24], nac, ALU.add)
            PS.put(b, u)
            yield from at
            yield
            mflush()
            take = feed((W[:, 768:1280], 8, 512), (W[:, 1280:1792], 8, 512), (W[:, 1792:2048], 8, 256),
                        (W[:, 0:512], 8, 512), (W[:, 512:768], 8, 256))
            if i == 0:
                V.op(lambda e: e.memset(XR[:, :, 0:3], 0.0))
            else:
                cp(V, XR[:, :, 0:3], TL, T.last(), A.last())
            yield
            held = None
            for j, n in ((0, 4), (4, 4), (8, 2), (-1, 512), (-2, 256), (None, 0)):
                if j is not None:
                    sl, v, tw = take()
                    if j >= 0:
                        b, t = chunks_tile(i, v, 0, n, tw)
                    else:
                        b = PS.get()
                        t = mm([(b[:, 0:n], [(Hi[c], v[:, c, 0:n]) for c in range(8)])], tw, b.free)
                    sl.free = [t]
                if held is not None:
                    j_, n_, b_, t_ = held
                    if j_ >= 0:
                        u = cp(A, XR[:, j_:j_ + n_, 3:131], b_[:, 0:128 * n_].rearrange("p (k t) -> p k t", k=n_),
                               t_, V.last())
                    else:
                        c0 = 0 if j_ == -1 else 512
                        u = act(ZT[:, c0:c0 + n_], b_[:, 0:n_], ACT.Silu, t_, V.last())
                    PS.put(b_, u)
                held = (j, n, b, t)
                if j is not None:
                    yield
            tz = A.last()
            k0 = PF["conv"][0]
            for c in range(10):
                def w_(k, c=c):
                    return pf[:, k0 + 10 * k + c:k0 + 10 * k + c + 1]
                ts(XC[:, c, :], XR[:, c, 0:128], w_(0), gain("convb", c), ALU.mult, ALU.add, tz, T.last())
                for k in range(1, 4):
                    t = stt(XC[:, c, :], XR[:, c, k:k + 128], w_(k), XC[:, c, :], ALU.mult, ALU.add)
                if c in (3, 6):
                    yield
            if i == 0:
                cp(V, TL, XR[:, :, 128:131])
            t = act(XC, XC, ACT.Silu, t)
            yield
            got = []
            for c in range(0, 6, 4):
                m = min(4, 6 - c)
                b = PS.get()
                u = tr([(b[:, 128 * k:128 * k + 128], XC[:, c + k, :]) for k in range(m)], t, b.free)
                got.append((b, u, c, m))
            lo = 128 * (1 - i)
            cb = PS.get()
            for g in range(2):
                jobs = [(cb[:, 256 * g + 128:256 * g + 256], [(XC[:, 6 + g, :], XC[:, 8 + g, :])])]
                if i == 1:
                    jobs.append((cb[:, 256 * g:256 * g + 128], [(B0[:, g, :], XC[:, 8 + g, :])]))
                tcb = mm(jobs, cb.free)
            yield
            for b, u, c, m in got:
                PS.put(b, cp(A, XS[:, 128 * c:128 * (c + m)], b[:, 0:128 * m], u, V.last()))
            PS.put(cb, cp(V, CB[:, :, lo:256], cb[:, :].rearrange("p (g n) -> p g n", g=2)[:, :, lo:256], tcb, A.last()))
            if i == 0:
                cp(V, B0, XC[:, 6:8, :])
            yield
            tt(V, XD[:, i, :].rearrange("p (s d) -> p s d", s=12), XS.rearrange("p (s d) -> p s d", s=12),
               dt.unsqueeze(2).to_broadcast([P, 12, 64]), ALU.mult, A.last())
            yb = [PS.get(), PS.get()]
            efree = [[T.last(), V.last()], [T.last(), V.last()]]
            pend, ahead = None, None
            for hp in range(8):
                if ahead is not None:
                    hp_, b, u = ahead
                    k = hp_ % 2
                    x = tt(V, TM[:, k], b[:, 0:256].rearrange("p (h n) -> p h n", h=2),
                           C("mt").unsqueeze(1).to_broadcast([P, 2, 128]), ALU.add, u, A.last())
                    for n in range(2):
                        h = 2 * hp_ + n
                        if i == 1:
                            act(EE[:, k, n, 0:128], b[:, 128 * n:128 * n + 128], ACT.Exp, x, efree[k],
                                bias=eb[:, h:h + 1])
                        t = act(EE[:, k, n, 128:256], TM[:, k, n, :], ACT.Exp, x, efree[k], bias=nac[:, h:h + 1])
                    PS.put(b, t)
                    new = (k, hp_, t)
                else:
                    new = None
                if hp < 6:
                    b = PS.get()
                    u = mm([(b[:, 128 * n:128 * n + 128],
                             [(da[:, 2 * hp + n:2 * hp + n + 1].to_broadcast([P, 128]), C("uinc"))])
                            for n in range(2)], b.free)
                    ahead = (hp, b, u)
                else:
                    ahead = None
                if pend is not None:
                    yield
                    k_, hp_, t_ = pend
                    x = tt(V, EE[:, k_, :, lo:256], EE[:, k_, :, lo:256],
                           CB[:, hp_ // 3, lo:256].unsqueeze(1).to_broadcast([P, 2, 256 - lo]), ALU.mult, t_)
                    jobs = []
                    for n in range(2):
                        h = 2 * hp_ + n
                        pr = [(EE[:, k_, n, 0:128], XD[:, 0, 64 * h:64 * h + 64])] if i == 1 else []
                        pr.append((EE[:, k_, n, 128:256], XD[:, i, 64 * h:64 * h + 64]))
                        jobs.append((yb[h // 8][:, 64 * (h % 8):64 * (h % 8) + 64], pr))
                    u = mm(jobs, x, yb[0].free, yb[1].free)
                    efree[k_] = [u]
                    tm_ = u
                pend = new
                yield
            take = feed(*[(I["w_o_2"][1][:, 512 * n:512 * n + 512], 8, 512) for n in range(2)])
            tt(V, TR.rearrange("p (s d) -> p s d", s=12), XS.rearrange("p (s d) -> p s d", s=12),
               B("dskip").unsqueeze(2).to_broadcast([P, 12, 64]), ALU.mult)
            for j, n in ((0, 512), (1, 256)):
                x = tt(V, TR[:, 512 * j:512 * j + n], TR[:, 512 * j:512 * j + n], yb[j][:, 0:n], ALU.add, tm_)
                PS.put(yb[j], x)
            tt(V, TR, TR, ZT, ALU.mult, tz)
            r, t = rstd_row(TR, 768, Y[:, i, 0:768])
            t = act(Y[:, i, 0:768], TR, ACT.Copy, t, scale=r)
            yield from turn_tile(i, [(Y[:, i, 0:768], 0, 6, "outn"), (OM[:, i, :], 6, 2, None)], t, V.last())
            yield from residual_tile(i, take)

        def top16(tsv, tiv, src, scratch, w=None):
            V.op(lambda e: e.max(tsv[:, 0:8], src), w)
            V.op(lambda e: e.max_index(tiv[:, 0:8], tsv[:, 0:8], src))
            V.op(lambda e: e.match_replace(scratch, tsv[:, 0:8], src, LOW))
            V.op(lambda e: e.max(tsv[:, 8:16], scratch))
            return V.op(lambda e: e.max_index(tiv[:, 8:16], tsv[:, 8:16], scratch))

        done_ix = {}

        def route(l, i, q, tq, tks):
            SS = ar[:, 4352:4864].rearrange("p (c n) -> p c n", c=4)
            CA = ar[:, 4864:5376].rearrange("p (h n) -> p h n", h=2)
            EQ = ar[:, 5376:5888]
            R2 = ar[:, 5888:6144]
            TS = ar[:, 6144:6208].rearrange("p (c n) -> p c n", c=4)
            TIU = arU[:, 6208:6272].rearrange("p (c n) -> p c n", c=4)
            TIF = ar[:, 6272:6336].rearrange("p (c n) -> p c n", c=4)
            BS = ar[:, 6336:6368].rearrange("p (h n) -> p h n", h=2)
            PO = arU[:, 6368:6400].rearrange("p (h n) -> p h n", h=2)
            PQ = arU[:, 6400:6464].rearrange("p (s h n) -> p s h n", s=2, h=2)
            PF_ = ar[:, 6464:6528].rearrange("p (s h n) -> p s h n", s=2, h=2)
            I12 = ar[:, 6528:6592].rearrange("p (s h n) -> p s h n", s=2, h=2)
            sums = small(16, 2)
            b = PS.get()
            t = mm([(b[:, 128 * k:128 * k + 128], [(QT[:, 4 * q + k, 128 * i:128 * i + 128], KS[l][:, k % 2, :])])
                    for k in range(4)], tq, tks, b.free)
            yield
            u = cp(A, SS, b[:, :].rearrange("p (k n) -> p k n", k=4), t, V.last())
            PS.put(b, u)
            yield
            for c in range(4):
                top16(TS[:, c, :], TIU[:, c, :], SS[:, c, :], R2[:, 0:128], u)
                yield
            cp(V, TIF, TIU)
            t4 = TS.rearrange("p (h i) n -> p h i n", i=2)
            tt(V, CA.rearrange("p h (a b) -> p h a b", a=16), t4[:, :, 0, :].unsqueeze(3).to_broadcast([P, 2, 16, 16]),
               t4[:, :, 1, :].unsqueeze(2).to_broadcast([P, 2, 16, 16]), ALU.add)
            yield
            for h in range(2):
                top16(BS[:, h, :], PO[:, h, :], CA[:, h, :], R2[:, 0:256])
                yield
            gi = GA[:, i, 32 * q:32 * q + 32].rearrange("p (h n) -> p h n", h=2)
            t = tt(V, gi, BS, BS[:, :, 0:1].to_broadcast([P, 2, 16]), ALU.subtract)
            t = act(gi, gi, ACT.Exp, t)
            ts(PQ[:, 0], PO, 4, None, ALU.logical_shift_right, None)
            ts(PQ[:, 1], PO, 15, None, ALU.bitwise_and, None)
            cp(V, PF_, PQ)
            yield
            f4 = TIF.rearrange("p (h i) n -> p h i n", i=2)
            io = C("iota")[:, 0:16].unsqueeze(1).unsqueeze(1).to_broadcast([P, 2, 16, 16])
            e4 = EQ.rearrange("p (h k a) -> p h k a", h=2, k=16)
            for n in range(2):
                tt(V, e4, PF_[:, n].unsqueeze(3).to_broadcast([P, 2, 16, 16]), io, ALU.is_equal)
                tt(V, e4, e4, f4[:, :, n, :].unsqueeze(2).to_broadcast([P, 2, 16, 16]), ALU.mult)
                red(I12[:, n], e4, ALU.add)
                yield
            stt(I12[:, 0], I12[:, 0], 128.0, I12[:, 1], ALU.mult, ALU.add)
            done_ix[(l, i, q)] = ts(IX[:, i, 32 * q:32 * q + 32].rearrange("p (h n) -> p h n", h=2), I12[:, 0],
                                    float(l * 16384), None, ALU.add, None)
            red(sums, gi, ALU.add, t)
            recip(sums, sums)
            tt(V, gi, gi, sums.unsqueeze(2).to_broadcast([P, 2, 16]), ALU.mult)
            yield

        tqs, tkss = {}, {}

        def prep_both():
            last = [T.last(), V.last(), A.last(), G.last()]
            tkss[0] = one[7].load(S, [(KS[0], I["sk"][0])], *last)
            tg = bcast_row("ffn20", gb, one[8], *last)
            th = norm("ffn20")
            for i in range(2):
                tt(V, Y[:, i, :], Y[:, i, :], gb, ALU.mult, tg, A.last(), T.last())
            for j in range(4):
                tile = wload(I["peer_w_q_2"][0][:, 512 * j:512 * j + 512], 8, 512)
                t, tqs[(0, j)] = proj_T(tile, cols, 4, 8, HT,
                                        lambda a, m, j=j: (QT[:, 4 * j + a:4 * j + a + m, :], 1.0), th)
                tile[0].free = [t]
                if j == 0:
                    drain(route(0, 0, 0, tqs[(0, 0)], tkss[0]))

        routes_done = [True]

        def prep_tile(i):
            if i == 0:
                tkss[1] = one[9].load(S, [(KS[1], I["sk"][1])])
                tkss["g"] = bcast_row("ffn21", gb, one[8], V.last())
            take = feed(*[(I["peer_w_q_2"][1][:, 512 * j:512 * j + 512], 8, 512) for j in range(4)])
            yield from norm_tile(i, "ffn21")
            th = [V.last(), A.last()]
            tt(V, Y[:, i, :], Y[:, i, :], gb, ALU.mult, tkss["g"], A.last(), T.last())
            held = None
            for j in range(5):
                if j < 4:
                    sl, v, tw = take()
                    b, t = chunks_tile(i, v, 0, 4, [tw, th])
                    sl.free = [t]
                if held is not None:
                    j_, b_, t_ = held
                    u = cp(A, QT[:, 4 * j_:4 * j_ + 4, 128 * i:128 * i + 128],
                           b_[:, :].rearrange("p (k t) -> p k t", k=4), t_)
                    PS.put(b_, u)
                    tqs[(1, j_)] = [u]
                held = (j, b, t)
                if j < 4:
                    yield
            while not routes_done[0]:
                yield
            yield from route(1, i, 0, tqs[(1, 0)], tkss[1])

        dgfree = [[] for _ in range(4)]
        rows = (I["pu"], I["pv"])

        def stage(l, i, after, side, rate):
            acc = [PS.get(), PS.get()]
            routes_done[0] = False
            for q in range(4):
                if q < 3:
                    nxt = route(l, i, q + 1, tqs[(l, q + 1)], tkss[l])
                elif after is not None:
                    nxt = route(l, after, 0, tqs[(l, 0)], tkss[l])
                else:
                    nxt = iter(())
                    routes_done[0] = True
                for jb in range(16 * q, 16 * q + 16):
                    sl = WR.get()
                    G.wait(sl.free, done_ix[(l, i, q)])
                    bufs = sl.buf.rearrange("p (k n) -> p k n", k=4)
                    for k in range(4):
                        def f(e, k=k, jb=jb, bufs=bufs, sl=sl):
                            e.indirect_dma_start(
                                out=bufs[:, k, :], out_offset=None, in_=rows[k // 2],
                                in_offset=bass.IndirectOffsetOnAxis(ap=IX[:, i, 2 * jb + k % 2:2 * jb + k % 2 + 1], axis=0),
                            ).then_inc(sl.gsem, 16)
                        G.items.append(f)
                    sl.gcnt += 64
                    tok = (sl.gsem, sl.gcnt)
                    for k in range(2):
                        j = 2 * jb + k
                        t = ttr(JK, bufs[:, k, :], Y[:, i, :], ALU.mult, ALU.add, 0.0, DT[:, i, j:j + 1], tok)
                    tge = act(DT[:, i, 2 * jb:2 * jb + 2], DT[:, i, 2 * jb:2 * jb + 2], ACT.Gelu, t)
                    next(nxt, None)
                    if jb % 2 and not rate:
                        next(nxt, None)
                    for _ in range(rate):
                        next(side, None)
                    for k in range(2):
                        j = 2 * jb + k
                        d = DG[:, j % 4, :]
                        u = ts(d, ident, DT[:, i, j:j + 1], GA[:, i, j:j + 1], ALU.mult, ALU.mult, tge, dgfree[j % 4])

                        def g(e, j=j, d=d, k=k, bufs=bufs, acc=acc):
                            for n in range(2):
                                m = e.matmul(acc[n][:, :], d, bufs[:, 2 + k, 512 * n:512 * n + 512],
                                             start=(j == 0), stop=(j == 127))
                            return m
                        x = T.op(g, u, tok, acc[0].free, acc[1].free)
                        dgfree[j % 4] = [x]
                    sl.free = [x]
                drain(nxt)
            drain(side)
            for n in range(2):
                xs = X[:, i, 512 * n:512 * n + 512]
                PS.put(acc[n], tt(V, xs, xs, acc[n][:, :], ALU.add, x))

        def final_tile(i):
            if i == 0:
                tkss["f"] = bcast_row("final2", gb, one[11], V.last())
                yield
                yield
            r, t = rstd_row(X[:, i, :], 1024, Y[:, i, :])
            yield
            t = stt(Y[:, i, :], X[:, i, :], r, gb, ALU.mult, ALU.mult, tkss["f"], A.last())
            S.wait(t)
            S.items.append(lambda e: e.dma_start(out[0, 128 * i:128 * i + 128, :], Y[:, i, :]).then_inc(s_out, 16))
            yield

        def beside(i):
            yield from mix_b(i)
            yield from prep_tile(i)

        for l in range(2):
            mixer(l)
            experts(l, memory() if l else rel_tables())
        row_norm("final", X, one[9])
        mix_a(zt, [V.last(), A.last()])
        prep_both()
        stage(0, 0, 1, iter(()), 0)
        stage(0, 1, None, beside(0), 1)
        stage(1, 0, None, beside(1), 1)
        stage(1, 1, None, final_tile(0), 1)
        drain(final_tile(1))
        S.items.append(lambda e: e.wait_ge(s_out, 32))


        block = ctx.enter_context(nc.Block())

        @block.sync
        def _(e):
            S.play(e)

        @block.gpsimd
        def _(e):
            G.play(e)

        @block.scalar
        def _(e):
            A.play(e)

        @block.vector
        def _(e):
            V.play(e)

        @block.tensor
        def _(e):
            T.play(e)


def _constants():
    import numpy as np
    f = np.float32
    p = np.arange(128)[:, None]
    dist = p - np.arange(384)[None, :] + 128
    ad = np.abs(dist).astype(f)

    def slopes(n):
        return (2.0 ** (-8.0 * np.arange(1, n + 1) / n)).astype(f)

    masks = [ad <= 64, dist % 4 == 0, dist % 16 == 0]
    sd, sw = slopes(12), slopes(16)
    cd = np.zeros((4, 128, 3, 384), f)
    for s in range(4):
        for g in range(3):
            cd[s, :, g] = np.where(masks[g], -sd[4 * g + s] * ad, f(NEG))
    cw = np.zeros((4, 128, 4, 384), f)
    for h in range(16):
        cw[h // 4, :, h % 4] = np.where(ad <= 128, -sw[h] * ad, f(NEG))
    n = np.maximum(255 - np.arange(511), 0)
    nf = np.maximum(n, 16).astype(f)
    large = 16 + (np.log(nf / 16) / f(np.log(8.0)) * 16).astype(np.int32)
    bucket = np.where(n < 16, n, np.minimum(large, 31))
    oh = (bucket[None, :] == np.arange(32)[:, None]).astype(f)
    co = np.zeros((128, CO["all"][1]), f)

    def put(name, a):
        co[:, CO[name][0]:CO[name][1]] = a

    q = np.arange(128)[None, :]
    put("ident", p == q)
    put("uinc", p <= q)
    put("ustr", p < q)
    put("ones", 1.0)
    k = np.arange(256)[None, :]
    put("causal", np.concatenate([np.where(k <= p + 128 * i, 0.0, NEG) for i in range(2)], axis=1))
    put("mt", np.where(p <= q, 0.0, NEG))
    put("iota", np.arange(32)[None, :])
    put("nhalf", -0.5)
    return {"cd": cd.reshape(4, 128, 1152), "cw": cw.reshape(4, 128, 1536), "oh": oh, "co": co}


def _arrays(inputs):
    import numpy as np
    g = {k: np.asarray(v) for k, v in inputs.items()}
    a = {k: np.ascontiguousarray(g[k]) for k in (
        "x", "w_branch_a", "w_branch_b", "w_out", "w_router", "w_expert_gate", "w_expert_up", "w_expert_down",
        "mem_2", "rel_bias_2", "w_o_2", "w_mem_kv_2", "a_w_in_2", "b_w_in_2", "peer_w_q_2")}
    a.update(_constants())
    w = g["w_in"]
    qw = w[:, :, 2304:3328].reshape(2, 1024, 2, 2, 4, 64).transpose(0, 1, 2, 4, 3, 5).reshape(2, 1024, 1024)
    a["w_in"] = np.ascontiguousarray(np.concatenate([w[:, :, :2304], qw, w[:, :, 3328:]], axis=2))

    def col(v):
        return v.reshape(-1, 128).T

    pf = [col(g["norm_mix"][0]), col(g["norm_mix"][1]), col(g["norm_ffn"][0]), col(g["norm_ffn"][1]),
          col(g["mix_norm_2"][0]), col(g["mix_norm_2"][1]), col(g["ffn_norm_2"][0]), col(g["ffn_norm_2"][1]),
          col(g["mem_norm_2"]), col(g["b_gate"][0]), col(g["b_gate"][1])]
    pf += [col(g["b_conv_w_2"][0, k]) for k in range(4)]
    pf += [col(g["b_conv_b_2"][0]), col(g["a_kv_norm_2"][0]), col(g["b_out_norm_2"][0])]
    a["pf"] = np.ascontiguousarray(np.concatenate(pf, axis=1))
    pr = [g["norm_final"], g["final_norm_2"], g["ffn_norm_2"][0], g["ffn_norm_2"][1], g["a_kv_norm_2"][0],
          g["sink_logit"][0], g["sink_logit"][1], g["b_dt_bias_2"][0], g["b_a_log_2"][0], g["b_d_skip_2"][0]]
    pr = np.concatenate(pr)
    a["pr"] = np.ascontiguousarray(pr.reshape(1, -1))
    a["uk"] = np.ascontiguousarray(g["a_w_uk_2"][0].transpose(1, 0, 2).reshape(256, 768))
    a["uv"] = np.ascontiguousarray(g["a_w_uv_2"][0].transpose(1, 0, 2).reshape(256, 768))
    a["sk"] = np.ascontiguousarray(g["peer_sub_keys_2"].transpose(0, 3, 1, 2))
    a["pu"] = np.ascontiguousarray(g["peer_u_2"]).reshape(32768, 1024)
    a["pv"] = np.ascontiguousarray(g["peer_v_2"]).reshape(32768, 1024)
    return a


def kernel(**inputs):
    import numpy as np
    import concourse.bacc as bacc
    from concourse.bass_utils import run_bass_kernel_spmd

    nc = bacc.Bacc("TRN2", target_bir_lowering=False, num_devices=1)
    arrays, I = {}, {}
    for name, v in _arrays(inputs).items():
        arrays[f"in_{name}"] = v
        I[name] = nc.dram_tensor(f"in_{name}", v.shape, mybir.dt.from_np(v.dtype), kind="ExternalInput").ap()
    out = nc.dram_tensor("out_0", (1, 256, 1024), F32, kind="ExternalOutput").ap()
    program(nc, I, out)
    r = run_bass_kernel_spmd(nc, [arrays], core_ids=[0])
    return r.results[0]["out_0"]
```
